# Optimizing a Trainium2 kernel written in Bass

```python
import jax, jax.numpy as jnp
from jax import lax
import numpy as np
import math
import jax
import jax.numpy as jnp

D_MODEL = 1024
BATCH = 1
SEQ = 512
DEPTH = 1

CONV_CH = 512
CONV_WIDTH = 31
N_HEADS = 8
N_KV_HEADS = 2
HEAD_DIM = 64
WINDOW = 128
ATTN_BLOCK = 128
N_GROUPS = 4
EXPERTS_PER_GROUP = 8
N_EXPERTS = N_GROUPS * EXPERTS_PER_GROUP
EXPERT_TOP_K = 2
D_FF_EXPERT = 512
MOE_BLOCK = 128
NORM_EPS = 1e-6

Q_DIM = N_HEADS * HEAD_DIM
KV_DIM = N_KV_HEADS * HEAD_DIM
IN_COLS = 2 * CONV_CH + Q_DIM + 2 * KV_DIM + 2 * D_MODEL


def rms_norm(x, g):
    xf = x.astype(jnp.float32)
    y = xf * lax.rsqrt(jnp.mean(xf * xf, axis=-1, keepdims=True) + NORM_EPS)
    return (y * g.astype(jnp.float32)).astype(x.dtype)

def layer_norm(x, g, b):
    xf = x.astype(jnp.float32)
    mu = jnp.mean(xf, axis=-1, keepdims=True)
    var = jnp.mean(jnp.square(xf - mu), axis=-1, keepdims=True)
    y = (xf - mu) * lax.rsqrt(var + NORM_EPS)
    return (y * g.astype(jnp.float32) + b.astype(jnp.float32)).astype(x.dtype)

def alibi_slopes():
    return jnp.asarray(np.array([2.0 ** (-8.0 * (h + 1) / N_HEADS) for h in range(N_HEADS)], np.float32))

def conformer_conv(u, w_dw, b_dw, ln_g, ln_b):
    a, gate = jnp.split(u, 2, axis=-1)
    v = a * jax.nn.sigmoid(gate)
    y = lax.conv_general_dilated(
        v, w_dw, window_strides=(1,), padding=[(CONV_WIDTH - 1, 0)],
        dimension_numbers=("NWC", "WIO", "NWC"), feature_group_count=CONV_CH)
    y = y + b_dw
    return jax.nn.silu(layer_norm(y, ln_g, ln_b))

def sliding_window_attention(q, k, v, sinks):
    b, s = q.shape[0], q.shape[1]
    nb = s // ATTN_BLOCK
    grp = N_HEADS // N_KV_HEADS
    qb = q.reshape(b, nb, ATTN_BLOCK, N_KV_HEADS, grp, HEAD_DIM)
    kb = k.reshape(b, nb, ATTN_BLOCK, N_KV_HEADS, HEAD_DIM)
    vb = v.reshape(b, nb, ATTN_BLOCK, N_KV_HEADS, HEAD_DIM)

    def with_prev(t):
        prev = jnp.pad(t[:, :-1], ((0, 0), (1, 0), (0, 0), (0, 0), (0, 0)))
        return jnp.concatenate([prev, t], axis=2)

    kk, vv = with_prev(kb), with_prev(vb)
    scores = jnp.einsum("bnqhgd,bnkhd->bnhgqk", qb, kk,
                        preferred_element_type=jnp.float32) * (HEAD_DIM ** -0.5)
    qi = jnp.arange(ATTN_BLOCK)[:, None]
    kj = jnp.arange(2 * ATTN_BLOCK)[None, :]
    rel = ATTN_BLOCK + qi - kj
    in_window = (rel >= 0) & (rel < WINDOW)
    key_exists = (jnp.arange(nb)[:, None, None] * ATTN_BLOCK + kj[None] - ATTN_BLOCK) >= 0
    mask = in_window[None] & key_exists
    slopes = alibi_slopes().reshape(N_KV_HEADS, grp)
    scores = scores - slopes[:, :, None, None] * rel.astype(jnp.float32)
    scores = jnp.where(mask[None, :, None, None], scores, -jnp.inf)
    sink = sinks.astype(jnp.float32).reshape(N_KV_HEADS, grp)[None, None, :, :, None, None]
    m = jnp.maximum(jnp.max(scores, axis=-1, keepdims=True), sink)
    p = jnp.exp(scores - m)
    p = p / (jnp.sum(p, axis=-1, keepdims=True) + jnp.exp(sink - m))
    out = jnp.einsum("bnhgqk,bnkhd->bnqhgd", p.astype(v.dtype), vv)
    return out.reshape(b, s, Q_DIM)

def hierarchical_moe(xn, w_group, b_group, w_expert, b_expert, w_gate, w_up, w_down):
    b, s, d = xn.shape
    t = b * s
    xt = xn.reshape(t, d)
    g_logits = (xt @ w_group).astype(jnp.float32) + b_group.astype(jnp.float32)
    g_prob = jax.nn.softmax(g_logits, axis=-1)
    g_sel = jnp.argmax(g_logits, axis=-1).astype(jnp.int32)
    p_group = jnp.take_along_axis(g_prob, g_sel[:, None], axis=-1)[:, 0]
    e_logits = ((xt @ w_expert).astype(jnp.float32) + b_expert.astype(jnp.float32)).reshape(t, N_GROUPS, EXPERTS_PER_GROUP)
    e_in = jnp.take_along_axis(e_logits, g_sel[:, None, None], axis=1)[:, 0]
    top_val, top_idx = lax.top_k(e_in, EXPERT_TOP_K)
    weights = p_group[:, None] * jax.nn.softmax(top_val, axis=-1)
    expert_id = (g_sel[:, None] * EXPERTS_PER_GROUP + top_idx.astype(jnp.int32)).reshape(-1)
    token_id = jnp.repeat(jnp.arange(t, dtype=jnp.int32), EXPERT_TOP_K)
    w_flat = weights.reshape(-1)
    n_assign = t * EXPERT_TOP_K
    n_blocks = -(-(n_assign + N_EXPERTS * (MOE_BLOCK - 1)) // MOE_BLOCK)
    order = jnp.argsort(expert_id, stable=True)
    sorted_e = expert_id[order]
    counts = jnp.zeros((N_EXPERTS,), jnp.int32).at[expert_id].add(1)
    padded = ((counts + MOE_BLOCK - 1) // MOE_BLOCK) * MOE_BLOCK
    padded_ends = jnp.cumsum(padded)
    padded_starts = padded_ends - padded
    starts = jnp.cumsum(counts) - counts
    rank = jnp.arange(n_assign, dtype=jnp.int32) - starts[sorted_e]
    dest = padded_starts[sorted_e] + rank
    slot_token = jnp.zeros((n_blocks * MOE_BLOCK,), jnp.int32).at[dest].set(token_id[order])
    slot_w = jnp.zeros((n_blocks * MOE_BLOCK,), jnp.float32).at[dest].set(w_flat[order])
    block_start = jnp.arange(n_blocks, dtype=jnp.int32) * MOE_BLOCK
    block_expert = jnp.clip(jnp.searchsorted(padded_ends, block_start, side="right"), 0, N_EXPERTS - 1).astype(jnp.int32)

    def run_block(args):
        tok, wt, e = args
        xb = xt[tok]
        hmid = jax.nn.silu(xb @ w_gate[e]) * (xb @ w_up[e])
        return (hmid @ w_down[e]) * wt[:, None].astype(xb.dtype)

    ys = lax.map(run_block, (slot_token.reshape(n_blocks, MOE_BLOCK),
                             slot_w.reshape(n_blocks, MOE_BLOCK), block_expert))
    out = jnp.zeros((t, d), xn.dtype).at[slot_token].add(ys.reshape(-1, d))
    return out.reshape(b, s, d)

def first_inputs(seed: int = 0) -> dict:
    key = jax.random.key(seed)
    ks = jax.random.split(key, 24)
    f32 = jnp.float32

    def nrm(k, shape, scale):
        return jax.random.normal(k, shape, f32) * scale

    L = DEPTH
    return {
        "x": jax.random.normal(ks[0], (BATCH, SEQ, D_MODEL), f32),
        "g_mix": 1.0 + nrm(ks[1], (L, D_MODEL), 0.02),
        "w_in": nrm(ks[2], (L, D_MODEL, IN_COLS), D_MODEL ** -0.5),
        "w_dw": nrm(ks[3], (L, CONV_WIDTH, 1, CONV_CH), CONV_WIDTH ** -0.5),
        "b_dw": nrm(ks[4], (L, CONV_CH), 0.02),
        "ln_conv_g": 1.0 + nrm(ks[5], (L, CONV_CH), 0.02),
        "ln_conv_b": nrm(ks[6], (L, CONV_CH), 0.02),
        "sinks": nrm(ks[7], (L, N_HEADS), 0.5),
        "w_conv_out": nrm(ks[8], (L, CONV_CH, D_MODEL), CONV_CH ** -0.5),
        "w_attn_out": nrm(ks[9], (L, Q_DIM, D_MODEL), Q_DIM ** -0.5),
        "w_out": nrm(ks[10], (L, D_MODEL, D_MODEL), D_MODEL ** -0.5),
        "g_ffn": 1.0 + nrm(ks[11], (L, D_MODEL), 0.02),
        "w_group": nrm(ks[12], (L, D_MODEL, N_GROUPS), D_MODEL ** -0.5),
        "b_group": nrm(ks[13], (L, N_GROUPS), 0.01),
        "w_expert": nrm(ks[14], (L, D_MODEL, N_EXPERTS), D_MODEL ** -0.5),
        "b_expert": nrm(ks[15], (L, N_EXPERTS), 0.01),
        "w_gate": nrm(ks[16], (L, N_EXPERTS, D_MODEL, D_FF_EXPERT), D_MODEL ** -0.5),
        "w_up": nrm(ks[17], (L, N_EXPERTS, D_MODEL, D_FF_EXPERT), D_MODEL ** -0.5),
        "w_down": nrm(ks[18], (L, N_EXPERTS, D_FF_EXPERT, D_MODEL), D_FF_EXPERT ** -0.5),
        "g_final": 1.0 + nrm(ks[19], (D_MODEL,), 0.02),
    }

def first_block(x, g_mix, w_in, w_dw, b_dw, ln_conv_g, ln_conv_b, sinks, w_conv_out, w_attn_out,
              w_out, g_ffn, w_group, b_group, w_expert, b_expert, w_gate, w_up, w_down, g_final):
    b, s, _ = x.shape
    cuts = list(np.cumsum([2 * CONV_CH, Q_DIM, KV_DIM, KV_DIM, D_MODEL]))
    h = x
    for l in range(DEPTH):
        xn = rms_norm(h, g_mix[l])
        proj = xn @ w_in[l]
        u_conv, q, k, v, gate_conv, gate_attn = jnp.split(proj, cuts, axis=-1)
        conv_o = conformer_conv(u_conv, w_dw[l], b_dw[l], ln_conv_g[l], ln_conv_b[l]) @ w_conv_out[l]
        attn = sliding_window_attention(q.reshape(b, s, N_HEADS, HEAD_DIM),
                                        k.reshape(b, s, N_KV_HEADS, HEAD_DIM),
                                        v.reshape(b, s, N_KV_HEADS, HEAD_DIM), sinks[l])
        attn_o = attn @ w_attn_out[l]
        merged = jax.nn.sigmoid(gate_conv) * conv_o + jax.nn.sigmoid(gate_attn) * attn_o
        h = h + merged @ w_out[l]
        h = h + hierarchical_moe(rms_norm(h, g_ffn[l]), w_group[l], b_group[l], w_expert[l],
                                 b_expert[l], w_gate[l], w_up[l], w_down[l])
    return rms_norm(h, g_final)


GDN_HEADS = 4
GDN_HEAD_DIM = 128
GDN_WIDTH = GDN_HEADS * GDN_HEAD_DIM
GDN_CONV = 4
GDN_CHUNK = 64
NSA_HEADS = 8
NSA_KV_GROUPS = 2
NSA_GROUP_HEADS = NSA_HEADS // NSA_KV_GROUPS
NSA_HEAD_DIM = 64
NSA_WIDTH = NSA_HEADS * NSA_HEAD_DIM
NSA_KV_WIDTH = NSA_KV_GROUPS * NSA_HEAD_DIM
CMP_BLOCK = 32
CMP_STRIDE = 16
CMP_HIDDEN = 128
SEL_BLOCK = 64
SEL_COUNT = 16
WINDOW_2 = 512
Q_BLOCK = 128
ROPE_THETA = 500000.0
ROPE_DIM = NSA_HEAD_DIM // 4
FORCED_SCORE = 1000.0
NEG_INF = -1e30
FFN_HIDDEN = -(-8 * D_MODEL // (3 * 256)) * 256
IN_SIZES = (3 * GDN_WIDTH, GDN_WIDTH, GDN_HEADS, GDN_HEADS,
            NSA_WIDTH, NSA_KV_WIDTH, NSA_KV_WIDTH, NSA_KV_WIDTH, NSA_KV_WIDTH, NSA_KV_WIDTH, NSA_KV_WIDTH,
            3 * NSA_HEADS, D_MODEL, D_MODEL)
IN_WIDTH = 4 * GDN_WIDTH + 2 * GDN_HEADS + NSA_WIDTH + 6 * NSA_KV_WIDTH + 3 * NSA_HEADS + 2 * D_MODEL


def rms_norm_2(x, gain):
    x32 = x.astype(jnp.float32)
    y = x32 * lax.rsqrt(jnp.mean(x32 * x32, axis=-1, keepdims=True) + NORM_EPS)
    return (y * gain.astype(jnp.float32)).astype(x.dtype)

def l2_normalize(x):
    return x * lax.rsqrt(jnp.sum(x * x, axis=-1, keepdims=True) + NORM_EPS)

def causal_depthwise_conv(x, w):
    k_len, ch = w.shape
    return lax.conv_general_dilated(x, w[:, None, :].astype(x.dtype), window_strides=(1,),
                                    padding=[(k_len - 1, 0)], dimension_numbers=('NWC', 'WIO', 'NWC'),
                                    feature_group_count=ch)

def partial_rope(x, pos):
    half = ROPE_DIM // 2
    inv_freq = ROPE_THETA ** (-jnp.arange(half, dtype=jnp.float32) / half)
    ang = pos.astype(jnp.float32)[:, None] * inv_freq
    bshape = (pos.shape[0],) + (1,) * (x.ndim - 3) + (half,)
    cos = jnp.cos(ang).reshape(bshape)
    sin = jnp.sin(ang).reshape(bshape)
    x1 = x[..., :half].astype(jnp.float32)
    x2 = x[..., half:ROPE_DIM].astype(jnp.float32)
    rot = jnp.concatenate([x1 * cos - x2 * sin, x2 * cos + x1 * sin], axis=-1).astype(x.dtype)
    return jnp.concatenate([rot, x[..., ROPE_DIM:]], axis=-1)

def gated_delta_rule_chunked(q, k, v, beta, g):
    b_, s_, h_, dk = q.shape
    dv = v.shape[-1]
    c = GDN_CHUNK
    n = s_ // c

    def to_chunks(a):
        return a.reshape(b_, n, c, h_, a.shape[-1]).transpose(0, 3, 1, 2, 4)

    q, k, v = to_chunks(q), to_chunks(k), to_chunks(v)
    beta = beta.reshape(b_, n, c, h_).transpose(0, 3, 1, 2)
    gc = jnp.cumsum(g.reshape(b_, n, c, h_).transpose(0, 3, 1, 2), axis=-1)
    causal = jnp.tril(jnp.ones((c, c), dtype=bool))
    strict = jnp.tril(jnp.ones((c, c), dtype=bool), -1)
    decay = jnp.exp(jnp.where(causal, gc[..., :, None] - gc[..., None, :], -jnp.inf))
    kb = k * beta[..., None]
    a_low = jnp.where(strict, jnp.einsum('bhnid,bhnjd->bhnij', kb, k) * decay, 0.0)
    ia = a_low + jnp.eye(c, dtype=q.dtype)
    u = lax.linalg.triangular_solve(ia, v * beta[..., None], left_side=True, lower=True, unit_diagonal=True)
    w = lax.linalg.triangular_solve(ia, kb * jnp.exp(gc)[..., None], left_side=True, lower=True, unit_diagonal=True)
    qk = jnp.einsum('bhnid,bhnjd->bhnij', q, k) * decay
    qg = q * jnp.exp(gc)[..., None]
    kd = k * jnp.exp(gc[..., -1:] - gc)[..., None]
    g_last = jnp.exp(gc[..., -1])

    def step(state, inp):
        qk_n, qg_n, kd_n, u_n, w_n, gl_n = inp
        v_new = u_n - jnp.einsum('bhcd,bhde->bhce', w_n, state)
        o_n = jnp.einsum('bhcd,bhde->bhce', qg_n, state) + jnp.einsum('bhij,bhje->bhie', qk_n, v_new)
        state = state * gl_n[..., None, None] + jnp.einsum('bhcd,bhce->bhde', kd_n, v_new)
        return state, o_n

    xs = tuple(jnp.moveaxis(a, 2, 0) for a in (qk, qg, kd, u, w, g_last))
    state0 = jnp.zeros((b_, h_, dk, dv), dtype=q.dtype)
    _, o = lax.scan(step, state0, xs)
    return o.transpose(1, 0, 3, 2, 4).reshape(b_, s_, h_, dv)

def compress_blocks(kv, pos_emb, w1, w2):
    s_ = kv.shape[1]
    n_cmp = (s_ - CMP_BLOCK) // CMP_STRIDE + 1
    idx = jnp.arange(n_cmp)[:, None] * CMP_STRIDE + jnp.arange(CMP_BLOCK)[None, :]
    blocks = kv[:, idx] + pos_emb[:, None, :]
    hid = jax.nn.silu(jnp.einsum('bnlgd,ldh->bgnh', blocks, w1))
    return jnp.einsum('bgnh,hd->bgnd', hid, w2)

def native_sparse_attention(q, k_cmp, v_cmp, k_slc, v_slc, k_win, v_win, gates,
                            cmp_pos_k, cmp_w1_k, cmp_w2_k, cmp_pos_v, cmp_w1_v, cmp_w2_v):
    b_, s_, g_, r_, dh = q.shape
    n_cmp = (s_ - CMP_BLOCK) // CMP_STRIDE + 1
    n_blk = s_ // SEL_BLOCK
    n_top = min(SEL_COUNT, n_blk)
    kc = compress_blocks(k_cmp, cmp_pos_k, cmp_w1_k, cmp_w2_k)
    vc = compress_blocks(v_cmp, cmp_pos_v, cmp_w1_v, cmp_w2_v)
    cmp_start = jnp.arange(n_cmp) * CMP_STRIDE
    cmp_end = cmp_start + CMP_BLOCK - 1
    blk_ids = jnp.arange(n_blk)
    sel_start = blk_ids * SEL_BLOCK
    overlap = ((cmp_start[:, None] <= sel_start[None, :] + SEL_BLOCK - 1)
               & (cmp_end[:, None] >= sel_start[None, :])).astype(jnp.float32)

    def to_blocks(a):
        return a.reshape(b_, n_blk, SEL_BLOCK, g_, dh).transpose(0, 3, 1, 2, 4).reshape(b_ * g_ * n_blk, SEL_BLOCK, dh)

    ks_flat = to_blocks(k_slc)
    vs_flat = to_blocks(v_slc)
    base = ((jnp.arange(b_)[:, None] * g_ + jnp.arange(g_)[None, :]) * n_blk)[:, :, None, None]
    pad = ((0, 0), (WINDOW_2, 0), (0, 0), (0, 0))
    kw_pad = jnp.pad(k_win, pad)
    vw_pad = jnp.pad(v_win, pad)
    span = WINDOW_2 + Q_BLOCK
    q_off = jnp.arange(Q_BLOCK)
    sel_off = jnp.arange(SEL_BLOCK)
    win_off = jnp.arange(span) - WINDOW_2

    def query_block(qi):
        s0 = qi * Q_BLOCK
        t = s0 + q_off
        qb = lax.dynamic_slice_in_dim(q, s0, Q_BLOCK, axis=1)
        gb = lax.dynamic_slice_in_dim(gates, s0, Q_BLOCK, axis=1)
        vis = cmp_end[None, :] <= t[:, None]
        sc = jnp.einsum('bqgrd,bgnd->bgrqn', qb, kc).astype(jnp.float32)
        p_cmp = jnp.where(vis, jax.nn.softmax(jnp.where(vis, sc, NEG_INF), axis=-1), 0.0)
        o_cmp = jnp.einsum('bgrqn,bgnd->bqgrd', p_cmp.astype(vc.dtype), vc)
        imp = jnp.einsum('bgrqn,nj->bgqj', p_cmp, overlap)
        cur = (t // SEL_BLOCK)[:, None]
        valid = blk_ids[None, :] <= cur
        forced = (blk_ids[None, :] == 0) | (blk_ids[None, :] == cur) | (blk_ids[None, :] == cur - 1)
        score = jnp.where(valid, jnp.where(forced, FORCED_SCORE, imp), -1.0)
        _, top = lax.top_k(score, n_top)
        flat = base + top
        s_list = []
        for s in range(n_top):
            kg = ks_flat[flat[..., s]]
            kpos = top[..., s, None] * SEL_BLOCK + sel_off
            sc_s = jnp.einsum('bqgrd,bgqkd->bgrqk', qb, kg).astype(jnp.float32)
            s_list.append(jnp.where((kpos <= t[:, None])[:, :, None], sc_s, NEG_INF))
        p_sel = jax.nn.softmax(jnp.concatenate(s_list, axis=-1), axis=-1).astype(vs_flat.dtype)
        o_sel = sum(jnp.einsum('bgrqk,bgqkd->bqgrd', p_sel[..., s * SEL_BLOCK:(s + 1) * SEL_BLOCK],
                               vs_flat[flat[..., s]]) for s in range(n_top))
        kw = lax.dynamic_slice_in_dim(kw_pad, s0, span, axis=1)
        vw = lax.dynamic_slice_in_dim(vw_pad, s0, span, axis=1)
        kpos_w = s0 + win_off
        rel = t[:, None] - kpos_w[None, :]
        ok = (rel >= 0) & (rel < WINDOW_2) & (kpos_w[None, :] >= 0)
        sc_w = jnp.einsum('bqgrd,bkgd->bgrqk', qb, kw).astype(jnp.float32)
        p_w = jax.nn.softmax(jnp.where(ok, sc_w, NEG_INF), axis=-1)
        o_win = jnp.einsum('bgrqk,bkgd->bqgrd', p_w.astype(vw.dtype), vw)
        return gb[..., 0:1] * o_cmp + gb[..., 1:2] * o_sel + gb[..., 2:3] * o_win

    out = lax.map(query_block, jnp.arange(s_ // Q_BLOCK))
    return out.transpose(1, 0, 2, 3, 4, 5).reshape(b_, s_, g_ * r_ * dh)

def hybrid_layer(x, pos, mix_norm_gain, w_in, gdn_conv_w, gdn_a_log, gdn_dt_bias, gdn_out_norm_gain,
                 cmp_pos_k, cmp_w1_k, cmp_w2_k, cmp_pos_v, cmp_w1_v, cmp_w2_v,
                 w_branch_gdn, w_branch_nsa, w_out, ffn_norm_gain, w_gate_up, w_down):
    f32 = jnp.float32
    b_, s_, _ = x.shape
    h = rms_norm_2(x, mix_norm_gain)
    proj = jnp.einsum('bsd,de->bse', h, w_in)
    split_at = np.cumsum(IN_SIZES)[:-1].tolist()
    (qkv_a, z_a, beta_a, alpha_a, q_b, kc_b, vc_b, ks_b, vs_b, kw_b, vw_b,
     gate_b, merge_a, merge_b) = jnp.split(proj, split_at, axis=-1)

    qkv_a = jax.nn.silu(causal_depthwise_conv(qkv_a, gdn_conv_w))
    q_a, k_a, v_a = [a.reshape(b_, s_, GDN_HEADS, GDN_HEAD_DIM).astype(f32) for a in jnp.split(qkv_a, 3, axis=-1)]
    q_a = l2_normalize(q_a) * (GDN_HEAD_DIM ** -0.5)
    k_a = l2_normalize(k_a)
    beta = jax.nn.sigmoid(beta_a.astype(f32))
    log_decay = -jnp.exp(gdn_a_log.astype(f32)) * jax.nn.softplus(alpha_a.astype(f32) + gdn_dt_bias.astype(f32))
    o_a = gated_delta_rule_chunked(q_a, k_a, v_a, beta, log_decay)
    o_a = (o_a * lax.rsqrt(jnp.mean(o_a * o_a, axis=-1, keepdims=True) + NORM_EPS)
           * gdn_out_norm_gain.astype(f32)
           * jax.nn.silu(z_a.astype(f32).reshape(b_, s_, GDN_HEADS, GDN_HEAD_DIM)))
    o_a = o_a.reshape(b_, s_, GDN_WIDTH).astype(x.dtype)

    q_n = partial_rope(q_b.reshape(b_, s_, NSA_KV_GROUPS, NSA_GROUP_HEADS, NSA_HEAD_DIM), pos) * (NSA_HEAD_DIM ** -0.5)
    kv_shape = (b_, s_, NSA_KV_GROUPS, NSA_HEAD_DIM)
    k_cmp = partial_rope(kc_b.reshape(kv_shape), pos)
    k_slc = partial_rope(ks_b.reshape(kv_shape), pos)
    k_win = partial_rope(kw_b.reshape(kv_shape), pos)
    gates = jax.nn.sigmoid(gate_b.reshape(b_, s_, NSA_KV_GROUPS, NSA_GROUP_HEADS, 3))
    o_b = native_sparse_attention(q_n, k_cmp, vc_b.reshape(kv_shape), k_slc, vs_b.reshape(kv_shape),
                                  k_win, vw_b.reshape(kv_shape), gates,
                                  cmp_pos_k, cmp_w1_k, cmp_w2_k, cmp_pos_v, cmp_w1_v, cmp_w2_v)

    merged = (jax.nn.sigmoid(merge_a) * jnp.einsum('bse,ed->bsd', o_a, w_branch_gdn)
              + jax.nn.sigmoid(merge_b) * jnp.einsum('bse,ed->bsd', o_b, w_branch_nsa))
    x = x + jnp.einsum('bsd,de->bse', merged, w_out)

    h2 = rms_norm_2(x, ffn_norm_gain)
    gate, up = jnp.split(jnp.einsum('bsd,df->bsf', h2, w_gate_up), 2, axis=-1)
    return x + jnp.einsum('bsf,fd->bsd', jax.nn.silu(gate) * up, w_down)

def second_inputs(seed: int = 0) -> dict:
    key = jax.random.key(seed)
    ks = jax.random.split(key, 24)
    f32 = jnp.float32
    L = DEPTH

    def nrm(k, shape, scale):
        return jax.random.normal(k, shape, f32) * scale

    def gain(k, shape):
        return 1.0 + 0.02 * jax.random.normal(k, shape, f32)

    dt = jnp.exp(jax.random.uniform(ks[5], (L, GDN_HEADS), f32, math.log(1e-3), math.log(1e-1)))
    return {
        'x': nrm(ks[0], (BATCH, SEQ, D_MODEL), 1.0),
        'mix_norm_gain': gain(ks[1], (L, D_MODEL)),
        'w_in': nrm(ks[2], (L, D_MODEL, IN_WIDTH), D_MODEL ** -0.5),
        'gdn_conv_w': nrm(ks[3], (L, GDN_CONV, 3 * GDN_WIDTH), GDN_CONV ** -0.5),
        'gdn_a_log': jnp.log(jax.random.uniform(ks[4], (L, GDN_HEADS), f32, 1.0, 16.0)),
        'gdn_dt_bias': dt + jnp.log(-jnp.expm1(-dt)),
        'gdn_out_norm_gain': gain(ks[6], (L, GDN_HEAD_DIM)),
        'cmp_pos_k': nrm(ks[7], (L, CMP_BLOCK, NSA_HEAD_DIM), 0.02),
        'cmp_w1_k': nrm(ks[8], (L, CMP_BLOCK, NSA_HEAD_DIM, CMP_HIDDEN), (CMP_BLOCK * NSA_HEAD_DIM) ** -0.5),
        'cmp_w2_k': nrm(ks[9], (L, CMP_HIDDEN, NSA_HEAD_DIM), CMP_HIDDEN ** -0.5),
        'cmp_pos_v': nrm(ks[10], (L, CMP_BLOCK, NSA_HEAD_DIM), 0.02),
        'cmp_w1_v': nrm(ks[11], (L, CMP_BLOCK, NSA_HEAD_DIM, CMP_HIDDEN), (CMP_BLOCK * NSA_HEAD_DIM) ** -0.5),
        'cmp_w2_v': nrm(ks[12], (L, CMP_HIDDEN, NSA_HEAD_DIM), CMP_HIDDEN ** -0.5),
        'w_branch_gdn': nrm(ks[13], (L, GDN_WIDTH, D_MODEL), GDN_WIDTH ** -0.5),
        'w_branch_nsa': nrm(ks[14], (L, NSA_WIDTH, D_MODEL), NSA_WIDTH ** -0.5),
        'w_out': nrm(ks[15], (L, D_MODEL, D_MODEL), D_MODEL ** -0.5),
        'ffn_norm_gain': gain(ks[16], (L, D_MODEL)),
        'w_gate_up': nrm(ks[17], (L, D_MODEL, 2 * FFN_HIDDEN), D_MODEL ** -0.5),
        'w_down': nrm(ks[18], (L, FFN_HIDDEN, D_MODEL), FFN_HIDDEN ** -0.5),
        'final_norm_gain': gain(ks[19], (D_MODEL,)),
    }

def second_block(x, mix_norm_gain, w_in, gdn_conv_w, gdn_a_log, gdn_dt_bias, gdn_out_norm_gain,
              cmp_pos_k, cmp_w1_k, cmp_w2_k, cmp_pos_v, cmp_w1_v, cmp_w2_v,
              w_branch_gdn, w_branch_nsa, w_out, ffn_norm_gain, w_gate_up, w_down, final_norm_gain):
    pos = jnp.arange(x.shape[1])
    for layer in range(DEPTH):
        x = hybrid_layer(x, pos, mix_norm_gain[layer], w_in[layer], gdn_conv_w[layer], gdn_a_log[layer],
                         gdn_dt_bias[layer], gdn_out_norm_gain[layer],
                         cmp_pos_k[layer], cmp_w1_k[layer], cmp_w2_k[layer],
                         cmp_pos_v[layer], cmp_w1_v[layer], cmp_w2_v[layer],
                         w_branch_gdn[layer], w_branch_nsa[layer], w_out[layer],
                         ffn_norm_gain[layer], w_gate_up[layer], w_down[layer])
    return rms_norm_2(x, final_norm_gain)


def setup_inputs(seed=0):
    out = dict(first_inputs(seed))
    for name, value in second_inputs(seed + 1).items():
        if name != "x":
            out[name + "_2"] = value
    return out


def reference(
    x, g_mix, w_in, w_dw, b_dw, ln_conv_g, ln_conv_b, sinks, w_conv_out, w_attn_out, w_out,
    g_ffn, w_group, b_group, w_expert, b_expert, w_gate, w_up, w_down, g_final, mix_norm_gain_2,
    w_in_2, gdn_conv_w_2, gdn_a_log_2, gdn_dt_bias_2, gdn_out_norm_gain_2, cmp_pos_k_2,
    cmp_w1_k_2, cmp_w2_k_2, cmp_pos_v_2, cmp_w1_v_2, cmp_w2_v_2, w_branch_gdn_2, w_branch_nsa_2,
    w_out_2, ffn_norm_gain_2, w_gate_up_2, w_down_2, final_norm_gain_2,
):
    x = first_block(
        x, g_mix, w_in, w_dw, b_dw, ln_conv_g, ln_conv_b, sinks, w_conv_out, w_attn_out, w_out,
        g_ffn, w_group, b_group, w_expert, b_expert, w_gate, w_up, w_down, g_final,
    )
    return second_block(
        x, mix_norm_gain_2, w_in_2, gdn_conv_w_2, gdn_a_log_2, gdn_dt_bias_2,
        gdn_out_norm_gain_2, cmp_pos_k_2, cmp_w1_k_2, cmp_w2_k_2, cmp_pos_v_2, cmp_w1_v_2,
        cmp_w2_v_2, w_branch_gdn_2, w_branch_nsa_2, w_out_2, ffn_norm_gain_2, w_gate_up_2,
        w_down_2, final_norm_gain_2,
    )


_drawn_inputs = setup_inputs


def setup_inputs(seed=0):
    import zlib

    import numpy as np

    out = dict(_drawn_inputs(seed))
    spreads = {}
    factors = {'g_mix': 3.058,
     'ln_conv_b': 3.007,
     'sinks': 4.038,
     'b_group': 8.911,
     'b_expert': 3.918,
     'mix_norm_gain_2': 4.753,
     'gdn_out_norm_gain_2': 7.884,
     'cmp_pos_k_2': 64.0,
     'cmp_pos_v_2': 64.0,
     'ffn_norm_gain_2': 13.988,
     'b_dw': 3.466}
    for name, (base, spread) in spreads.items():
        noise = np.random.default_rng([zlib.crc32(name.encode()), seed]).standard_normal(out[name].shape)
        drawn = base * np.exp(spread * noise) if base else spread * noise
        out[name] = jnp.asarray(drawn.astype(out[name].dtype))
    for name, factor in factors.items():
        out[name] = (out[name] * factor).astype(out[name].dtype)
    return out
```

```python
from contextlib import ExitStack

import concourse.bass as bass
from concourse import mybir

ALU = mybir.AluOpType
ACT = mybir.ActivationFunctionType
F32 = mybir.dt.float32
F32R = mybir.dt.float32r
I32 = mybir.dt.int32
U32 = mybir.dt.uint32
AX_X = mybir.AxisListType.X

P = 128
SEQ, D = 512, 1024
NT = SEQ // P
KD = D // P
EPS = 1e-6
NEG = -1e30

VEC = {}
_at = 0
for _name, _n in (("g_mix", 8), ("b_dw", 4), ("ln_g", 4), ("ln_b", 4), ("w_dw", 124), ("g_ffn", 8),
                  ("mix_gain", 8), ("conv2", 48), ("gdn_gain", 1), ("ffn_gain", 8), ("a_log", 1), ("dt_bias", 1)):
    VEC[_name] = (_at, _at + _n)
    _at += _n
NVEC = _at


class Stage:

    def __init__(self, slabs, tiles, elems=2048):
        self.slabs, self.tiles, self.elems = slabs, tiles, elems


STAGES = {
    "in1": Stage(7, 2), "gates1": Stage(8, 2), "attn_out": Stage(2, 4), "conv_out": Stage(2, 4), "out1": Stage(4, 4),
    "small2": Stage(1, 1, 1024), "in2q": Stage(8, 2), "in2n": Stage(5, 2), "in2m": Stage(8, 2), "gdn_out": Stage(2, 4), "nsa_out": Stage(2, 4), "out2": Stage(4, 4),
    "gate_up": Stage(22, 2), "down": Stage(11, 0),
}
ORDER = list(STAGES)
_s = 0
for _st in STAGES.values():
    _st.first = _s
    _s += _st.slabs

RING = {}
_t = 0
for _name, _n in (("xn1", 8), ("in1", 14), ("gates1", 16), ("attn_out", 8), ("conv_out", 8),
                  ("out1", 16), ("xnffn", 8), ("router", 1), ("router_t", 1), ("rank", 1),
                  ("xn2", 8), ("small2", 1), ("in2q", 16), ("in2n", 10), ("in2m", 16), ("gdn_out", 8), ("nsa_out", 8),
                  ("out2", 16), ("xnf", 8), ("gate_up", 44), ("down", 0), ("outT", 8)):
    RING[_name] = _t
    _t += _n


def freed(b, tiles):
    return (tiles + 1 - b) // 2


NE, NG, EPG, FF, BLK = 32, 4, 8, 512, 64
ASSIGN = 2 * SEQ
OVER = ASSIGN // BLK - 1
XS_ROWS = ASSIGN + BLK
YS_OVER = NE * BLK


USES = {}
_banks = [0] * 6


def _use(tag, bank):
    USES[tag] = (len(USES), bank, _banks[bank])
    _banks[bank] += 1


LEVELS = 6
CHUNK = 64
GH = 4
STEPS = [(i, g, hp, br) for i in range(NT) for g in range(2) for hp in range(2) for br in range(3)]


def chunks_T(i, br):
    return [[0]] if br == 0 else [list(range(a, min(a + 2, i + 1))) for a in range(0, i + 1, 2)]


for _k in range(8):
    _use(("l2", _k), _k % 2)
_use("smalltok", 2)
for _i in range(NT):
    for _tag, _b in (("gc", 0), ("beta", 1), ("ktok", 2), ("vtok", 3), ("AT", 4), ("QK", 5), ("D0", 0)):
        _use((_tag, _i), _b)
    for _l in range(1, LEVELS):
        _use(("P1", _i, _l), 1)
        if _l < LEVELS - 1:
            _use(("P2", _i, _l), 2)
        _use(("P3", _i, _l), 3)
    for _tag, _b in (("wT", 4), ("u", 5)):
        _use((_tag, _i), _b)
    for _a in range(2):
        _use(("V", _i, _a), 0)
        if _a == 1:
            _use(("O", _i), 1)
        _use(("S", _i, _a), 2)
    _use(("oT", _i), 3)
for _k in range(7):
    _use(("rope", _k), _k % 2)
for _tag, _b in (("vslc", 2), ("vwin", 3), ("hidk", 0), ("hidv", 1), ("kc", 4), ("vc", 5)):
    _use(_tag, _b)
for _n in range(2):
    _use(("sc", _n), 2 * _n)
    _use(("sc2", _n), 2 * _n + 1)
for _n, (_i, _g, _hp, _br) in enumerate(STEPS):
    for _c in range(len(chunks_T(_i, _br))):
        _use(("pT", _n, _c), 4)
        if _c == 0 and _n + 2 < len(STEPS):
            _use(("sc", _n + 2), 2 * (_n % 2))
            _use(("sc2", _n + 2), 2 * (_n % 2) + 1)
    if _br == 2 and _hp == 1:
        _use(("o", _i, _g), 5)


def each_slab(eng, name, body, peel=0, some=None):
    st = STAGES[name]
    if some != "rest":
        for j in range(min(peel, st.slabs)):
            body(j, (st.first + j) // 2, (st.first + j) % 2)
    if some == "peeled":
        return
    left = st.slabs - peel
    if left // 2 >= 2:
        with eng.Fori(0, left // 2) as i:
            for u in range(peel, peel + 2):
                body(2 * i + u, i + (st.first + u) // 2, (st.first + u) % 2)
    elif left >= 2:
        for j in range(peel, peel + 2 * (left // 2)):
            body(j, (st.first + j) // 2, (st.first + j) % 2)
    if left > 0 and left % 2:
        j = st.slabs - 1
        body(j, (st.first + j) // 2, (st.first + j) % 2)


def program(nc, t):
    with ExitStack() as ctx:
        def sem(name):
            return ctx.enter_context(nc.semaphore(name))

        here = [16512]

        def place(name, shape, dt, at=None):
            n = 4
            for x in shape[1:]:
                n *= x
            if at is None:
                at = here[0]
                here[0] = (at + n + 31) // 32 * 32
            x = nc.alloc_sbuf_tensor_at(name, shape, dt, offset=at)
            place.end = (at + n + 31) // 32 * 32
            return x

        vec = place("vec", [P, NVEC], F32)
        ident = place("ident", [P, P], F32)
        ones = place("ones", [P, P], F32)
        stat = place("stat", [P, 240], F32)
        zero = place("zero", [P, 128], F32)
        wr = place("wr", [P, KD, 36], F32)
        rbias = place("rbias", [P, 36], F32)
        tri = place("tri", [P, P], F32)
        one = place("one", [P, P], F32)
        desc = place("desc", [P, 32], F32)
        hres = place("hres", [P, NT, D], F32)
        raw = [place(f"raw{i}", [P, 2048], F32) for i in range(2)]
        whi = [place(f"whi{i}", [P, 2048], F32R) for i in range(2)]
        wlo = [place(f"wlo{i}", [P, 2048], F32R) for i in range(2)]
        act_at = here[0]
        acthi = place("acthi", [P, KD, SEQ], F32R)
        actlo = place("actlo", [P, KD, SEQ], F32R)
        a2_at = here[0]
        act2hi = place("act2hi", [P, KD, SEQ], F32R)
        act2lo = place("act2lo", [P, KD, SEQ], F32R)
        base = here[0]

        relneg = place("relneg", [P, 256], F32)
        proj = place("proj", [P, 30, SEQ], F32)
        proj_at = place.end - 30 * SEQ * 4
        vpad = place("vpad", [P, 4, 30 + SEQ], F32)
        kdup = place("kdup", [P, 2, SEQ], F32, at=a2_at + 24576)
        vtok = place("vtok", [P, NT, P], F32, at=a2_at + 28672)
        sinkb = place("sinkb", [P, 8], F32)
        xn = place("xn", [P, NT, D], F32, at=proj_at)
        sc = [place(f"sc{i}", [P, 4, 256], F32, at=a2_at + 4096 * i) for i in range(2)]
        pT = [place(f"pT{i}", [P, 2, SEQ], F32, at=a2_at + 8192 + 4096 * i) for i in range(2)]
        attnT = place("attnT", [P, 4, SEQ], F32, at=a2_at + 16384)
        assert here[0] <= 229344, here[0]

        here[0] = act_at
        wgu, wd, xg, xgT, hmT, yo = [], [], [], [], [], []
        for b in range(2):
            wgu.append(place(f"wgu{b}", [P, KD, 2 * FF], F32))
            wd.append(place(f"wd{b}", [P, FF // P, D], F32))
        xtT = place("xtT", [P, KD, SEQ], F32, at=act_at + 49152)
        for b in range(2):
            xg.append(place(f"xg{b}", [P, D // 2], F32))
            xgT.append(place(f"xgT{b}", [P, KD, BLK], F32))
            hmT.append(place(f"hmT{b}", [P, FF // P, BLK], F32))
            yo.append(place(f"yo{b}", [P, 512], F32))
        gb = place("gb", [P, D], F32)
        sg = place("sg", [P, 512], F32)
        hm = place("hm", [P, 512], F32)
        xt = place("xt", [P, NT, D], F32, at=act_at + 81920)
        rt = place("rt", [P, 16, 128], F32)
        idx = place("idx", [P, 64], U32)
        ovi = place("ovi", [P, 32], U32)
        ovt = place("ovt", [P, 16, NE], F32)
        assert here[0] <= 229344, here[0]
        yg = [place(f"yg{b}", [P, D], F32, at=act_at + 4096 * b) for b in range(8)]
        gfb = place("gfb", [P, D], F32, at=act_at + 32768)

        proj2_at = (229344 - 29 * SEQ * 4) // 32 * 32
        proj2 = place("proj2", [P, 29, SEQ], F32, at=proj2_at)
        smallT, smalltok = proj2[:, 27, :], proj2[:, 28, :].rearrange("p (i c) -> p i c", c=P)
        xn2 = place("xn2", [P, NT, D], F32, at=proj2_at)
        here[0] = a2_at
        gmask = place("gmask", [P, 2 + LEVELS, P], F32)
        sel = place("sel", [P, GH, P], F32)
        cgo = place("cgo", [P, SEQ], F32)

        def quads(name, at=None):
            return place(name, [P, GH, P], F32, at=at)
        S, Sg, ktok, vb, kbg, kd = [quads(n) for n in ("S", "Sg", "ktok", "vb", "kbg", "kd")]
        kbT_at = here[0]
        gcb_at, egc_at, decS_at, decI_at = [kbT_at + 2048 * n for n in (2, 3, 4, 5)]
        kbT, qgT, gcb, egc, decS, decI = [quads(n) for n in ("kbT", "qgT", "gcb", "egc", "decS", "decI")]
        AT, qkT, DT, Dm = [quads(n) for n in ("AT", "qkT", "DT", "Dm")]
        AL = [quads("AL0"), quads("AL1")]
        P1s, u_, vn = quads("P1s", kbT_at), quads("u_", decS_at), quads("vn", decI_at)
        nwT, on = quads("nwT", gcb_at), quads("on", egc_at)
        c4 = [place(f"c4_{b}", [P, SEQ], F32, at=a2_at + 12288 + 2048 * b) for b in range(2)]
        l2r = [place(f"l2r{b}", [P, SEQ], F32, at=a2_at + 16384 + 2048 * b) for b in range(2)]
        rowt = [place(f"rowt{b}", [P, SEQ], F32, at=kbT_at + 2048 * b) for b in range(2)]
        gdn_end = here[0]
        assert gdn_end <= proj2_at, (gdn_end, proj2_at)
        here[0] = a2_at
        cosT = place("cosT", [P, SEQ], F32)
        sinT = place("sinT", [P, SEQ], F32)
        rotp = place("rotp", [P, P], F32)
        dmask = place("dmask", [P, P], F32)
        cmask = place("cmask", [P, NT, 31], F32)
        rowvis = place("rowvis", [P, 1], F32)
        posT = place("posT", [P, 2, 16], F32)
        w2s = place("w2s", [P, 192], F32)
        rtmp = place("rtmp", [P, 2, SEQ], F32)
        kds = place("kds", [P, 2, SEQ], F32)
        kdw = place("kdw", [P, 2, SEQ], F32)
        vtS = place("vtS", [P, NT, P], F32)
        vtW = place("vtW", [P, NT, P], F32)
        kcd = place("kcd", [P, 2, 31], F32)
        vct = place("vct", [32, 2, 64], F32)
        hid = place("hid", [P, 2, 62], F32)
        w1_at = here[0]
        w1 = [place(f"w1_{b}", [P, 16, P], F32) for b in range(2)]
        blk = [place(f"blk{b}", [P, 16, 62], F32) for b in range(2)]
        assert here[0] <= proj2_at, (here[0], proj2_at)
        pr = [place(f"pr{b}", [P, 2, SEQ], F32, at=w1_at + 4096 * b) for b in range(2)]
        scale = [place(f"scale{b}", [P, 2, P], F32, at=w1_at + 16384 + 1024 * b) for b in range(2)]
        prT = [place(f"prT{b}", [P, 4, 2, P], F32, at=w1_at + 8192 + 4096 * b) for b in range(2)]
        xnf = place("xnf", [P, NT, D], F32, at=a2_at)
        here[0] = a2_at
        hhi = place("hhi", [P, 22, SEQ], F32R)
        hlo = place("hlo", [P, 22, SEQ], F32R)
        sgb = [place(f"sgb{b}", [P, SEQ], F32) for b in range(2)]
        hv = [place(f"hv{b}", [P, SEQ], F32) for b in range(2)]
        assert here[0] <= 229344
        outT = place("outT", [P, KD, SEQ], F32, at=act_at)
        fscr = place("fscr", [P, NT, D], F32, at=a2_at)
        goutb = place("goutb", [P, D], F32, at=act_at + 16384)
        fin = place("fin", [P, NT, D], F32, at=a2_at + 16384)
        xs_dram = nc.dram_tensor("xs_dram", [XS_ROWS, D], F32).ap()
        ys_dram = nc.dram_tensor("ys_dram", [YS_OVER + XS_ROWS, D], F32).ap()

        def vc(name, i=0, n=1):
            a = VEC[name][0] + i
            return vec[:, a:a + n]

        psg = ctx.enter_context(nc.psum_tensor("psg", [P, 2, 512], F32))
        psx = ctx.enter_context(nc.psum_tensor("psx", [P, 6, 512], F32))

        const_in = sem("const_in")
        x_in = sem("x_in")
        slab_loaded = [sem(f"slab_loaded{i}") for i in range(2)]
        slab_hi = sem("slab_hi")
        slab_lo = sem("slab_lo")
        tile_full = sem("tile_full")
        tile_free = [sem(f"tile_free{i}") for i in range(2)]
        ones_set = sem("ones_set")
        act_step = sem("act_step")
        dve_step = sem("dve_step")
        norm_ss = sem("norm_ss")
        norm_var = sem("norm_var")
        norm_sd = sem("norm_sd")
        norm_rs = sem("norm_rs")
        xn_made = sem("xn_made")
        hi_made = sem("hi_made")
        lo_made = sem("lo_made")
        conv_v = sem("conv_v")
        conv_tap = sem("conv_tap")
        conv_centred = sem("conv_centred")
        conv_sq = sem("conv_sq")
        conv_var = sem("conv_var")
        conv_sd = sem("conv_sd")
        conv_norm = sem("conv_norm")
        conv_act = sem("conv_act")
        conv_split = sem("conv_split")
        kdup_made = sem("kdup_made")
        scores_full = sem("scores_full")
        scores_read = sem("scores_read")
        negmax_made = sem("negmax_made")
        exps_made = sem("exps_made")
        probs_made = sem("probs_made")
        probsT_full = sem("probsT_full")
        probsT_copied = sem("probsT_copied")
        heads_full = sem("heads_full")
        heads_copied = sem("heads_copied")
        attn_hi = sem("attn_hi")
        attn_split = sem("attn_split")
        gates_sig = sem("gates_sig")
        vtok_full = sem("vtok_full")
        vtok_made = sem("vtok_made")
        mean_full = sem("mean_full")
        square_mean_full = sem("square_mean_full")
        merged_made = sem("merged_made")
        merged_hi = sem("merged_hi")
        merged_lo = sem("merged_lo")
        res_added = sem("res_added")
        gb_in = sem("gb_in")
        xt_made = sem("xt_made")
        route_act = sem("route_act")
        route_dve = sem("route_dve")
        logits_made = sem("logits_made")
        picks_made = sem("picks_made")
        dest_made = sem("dest_made")
        zero_set = sem("zero_set")
        tail_stored = sem("tail_stored")
        rows_scattered = sem("rows_scattered")
        gu_in = [sem(f"gu_in{b}") for b in range(2)]
        wd_in = [sem(f"wd_in{b}") for b in range(2)]
        xg_in = [sem(f"xg_in{b}") for b in range(2)]
        xgT_full = sem("xgT_full")
        xgT_made = sem("xgT_made")
        gu_full = sem("gu_full")
        hm_cleared = sem("hm_cleared")
        sg_made = sem("sg_made")
        hm_made = sem("hm_made")
        hmT_full = sem("hmT_full")
        hmT_made = sem("hmT_made")
        y_full = sem("y_full")
        yo_made = sem("yo_made")
        y_stored = [sem(f"y_stored{b}") for b in range(2)]
        o_in = sem("o_in")
        o_stored = sem("o_stored")
        over_done = sem("over_done")
        rows_gathered = [sem(f"rows_gathered{b}") for b in range(8)]
        combined = sem("combined")
        gf_in = sem("gf_in")
        x_full = sem("x_full")
        x_read = [sem(f"x_read{b}") for b in range(6)]
        final1_made = sem("final1_made")
        xn2_made = sem("xn2_made")
        xn2_hi = sem("xn2_hi")
        const2_in = sem("const2_in")
        small_act = sem("small_act")
        small_dve = sem("small_dve")
        rows_made = sem("rows_made")
        conv2_made = sem("conv2_made")
        l2_sq = sem("l2_sq")
        l2_made = sem("l2_made")
        gdn_pool = sem("gdn_pool")
        gdn_at = sem("gdn_at")
        gdn_done = sem("gdn_done")
        const3_in = sem("const3_in")
        sm_max = sem("sm_max")
        scale_made = sem("scale_made")
        nsa_done = sem("nsa_done")
        branch_hi = sem("branch_hi")
        branch_lo = sem("branch_lo")
        merged2_made = sem("merged2_made")
        merged2_hi = sem("merged2_hi")
        merged2_lo = sem("merged2_lo")
        x3_made = sem("x3_made")
        xnf_made = sem("xnf_made")
        xnf_hi = sem("xnf_hi")
        h_made = sem("h_made")
        h_hi = sem("h_hi")
        h_lo = sem("h_lo")
        down_used = sem("down_used")
        outT_made = sem("outT_made")
        x4_made = sem("x4_made")
        gout_in = sem("gout_in")
        out_made = sem("out_made")
        values_made = sem("values_made")
        gates2_made = sem("gates2_made")
        out_stored = sem("out_stored")

        SLOPES = [2.0 ** -(h + 1) for h in range(8)]

        def bank(tag):
            return psx[:, USES[tag][1], :]

        def begin(pe, tag):
            n, b, before = USES[tag]
            if before:
                pe.wait_ge(x_read[b], before)

        def filled(eng, tag):
            eng.wait_ge(x_full, USES[tag][0] + 1)

        def seen(tag):
            return x_read[USES[tag][1]]

        Q = {n: sem("gdn_" + n) for n in ("dec_in", "dec", "gle", "dsc_in", "dsc", "egc", "qgT", "scaled", "masked",
                                          "DT0", "vn", "S", "sq", "var", "sd", "on")}

        Q2 = {n: sem("nsa_" + n) for n in ("blk", "keys")}

        def gm(n):
            return gmask[:, n, :].unsqueeze(1).to_broadcast([P, GH, P])

        def slot(h):
            return 2 * (h % 2) + h // 2

        def slab_src(name, j):
            name_in, col = {"in1": ("w_in", 0), "gates1": ("w_in", 14 * P), "conv_out": ("w_conv_out", 0), "attn_out": ("w_attn_out", 0),
                            "out1": ("w_out", 0), "small2": ("w_small_2", 0), "in2q": ("w_in_2", 0),
                            "in2n": ("w_in_2", 2056), "in2m": ("w_in_2", 3360), "gdn_out": ("w_branch_gdn_2", 0),
                            "nsa_out": ("w_branch_nsa_2", 0), "out2": ("w_out_2", 0), "gate_up": ("w_gate_up_2", 0),
                            "down": ("w_down_2", 0)}[name]
            w = t[name_in]
            if name == "down":
                v = w.rearrange("(k p) c -> p k c", p=P)
                return [v[:, bass.ds(2 * j + h, 1), :] for h in range(2)], 2
            kt = 4 if STAGES[name].tiles == 4 and name[:3] != "out" else 8
            v = w.rearrange("(k p) c -> p k c", p=P)
            if name == "gate_up":
                return [v[:, :, bass.ds(2816 * h + P * j, P)] for h in range(2)], 8
            cols = STAGES[name].elems // kt
            return [v[:, h * kt // 2:(h + 1) * kt // 2, bass.ds(col + j * cols, cols)] for h in range(2)], kt

        def load_slabs(sp, name, peel=0, some=None):
            st = STAGES[name]

            def body(j, half, par):
                if not (isinstance(j, int) and st.first + j < 2):
                    sp.wait_ge(slab_lo, st.first + j - 1)
                srcs, kt = slab_src(name, j)
                dst = raw[par][:, 0:st.elems].rearrange("p (k c) -> p k c", k=kt)
                for h, src in enumerate(srcs):
                    part = dst[:, :, h * P:(h + 1) * P] if name == "gate_up" else dst[:, h * kt // 2:(h + 1) * kt // 2, :]
                    sp.dma_start(part, src).then_inc(slab_loaded[par], 16)
            each_slab(sp, name, body, peel, some)

        def slab_after(name, j):
            if j + 1 < STAGES[name].slabs:
                return name, j + 1
            k = ORDER.index(name) + 1
            return (ORDER[k], 0) if k < len(ORDER) else None

        def split_hi(act, elems, half, par, free):
            act.wait_ge(slab_loaded[par], 32 * half + 32)
            if not (isinstance(free, int) and free == 0):
                act.wait_ge(tile_full, free)
            act.activation(whi[par][:, 0:elems], raw[par][:, 0:elems], ACT.Copy).then_inc(slab_hi, 1)

        def split_slab_lo(pool, name, j, par):
            st = STAGES[name]
            pool.wait_ge(slab_hi, st.first + j + 1)
            pool.tensor_tensor(wlo[par][:, 0:st.elems], raw[par][:, 0:st.elems],
                               whi[par][:, 0:st.elems].bitcast(F32), ALU.subtract).then_inc(slab_lo, 1)

        def split_lo(pool, name, peel=0, some=None):
            each_slab(pool, name, lambda j, half, par: split_slab_lo(pool, name, j, par), peel, some)

        def slab_place(name, j):
            n = STAGES[name].first + j
            return n // 2, n % 2

        def half_of(base_tile, per, j):
            return base_tile // 2 + (per // 2) * j

        def next_hi(act, name, j, half, par):
            st = STAGES[name]
            free = RING[name] + st.tiles * j
            if isinstance(j, int):
                nxt = slab_after(name, j)
                if nxt is None:
                    return
                s = STAGES[nxt[0]].first + nxt[1]
                split_hi(act, STAGES[nxt[0]].elems, s // 2, s % 2, 0 if s < 2 else free)
            else:
                split_hi(act, st.elems, half + (1 if par else 0), 1 - par, free)

        def each_slab_act(act, name, body, peel=0):
            st = STAGES[name]

            def both(j, half, par):
                next_hi(act, name, j, half, par)
                body(j, half, par)
            last = 2 if (st.slabs - peel) % 2 == 0 else 1
            for j in range(min(peel, st.slabs)):
                both(j, (st.first + j) // 2, (st.first + j) % 2)
            turns = (st.slabs - peel - last) // 2
            if turns >= 2:
                with act.Fori(0, turns) as i:
                    for u in range(peel, peel + 2):
                        both(2 * i + u, i + (st.first + u) // 2, (st.first + u) % 2)
            elif turns > 0:
                for j in range(peel, peel + 2 * turns):
                    both(j, (st.first + j) // 2, (st.first + j) % 2)
            for j in range(max(peel, st.slabs - last), st.slabs):
                both(j, (st.first + j) // 2, (st.first + j) % 2)

        def features_by_tokens(pe, name, xhi, xlo, peel=0, after=None):
            st = STAGES[name]
            kt = 4 if st.tiles == 4 else 8

            def body(j, half, par):
                pe.wait_ge(slab_lo, st.first + j + 1)
                wh = whi[par][:, 0:st.elems].rearrange("p (k c) -> p k c", k=kt)
                wl = wlo[par][:, 0:st.elems].rearrange("p (k c) -> p k c", k=kt)
                for f in range(st.tiles):
                    b = (RING[name] + f) % 2
                    pe.wait_ge(tile_free[b], half_of(RING[name] + f, st.tiles, j))
                    c = slice(f * P, (f + 1) * P)
                    for k in range(kt):
                        pe.matmul(psg[:, b, :], wl[:, k, c], xhi[:, k, :], start=(k == 0), stop=False)
                        pe.matmul(psg[:, b, :], wh[:, k, c], xlo[:, k, :], start=False, stop=False)
                        mm = pe.matmul(psg[:, b, :], wh[:, k, c], xhi[:, k, :], start=False, stop=(k == kt - 1))
                    mm.then_inc(tile_full, 1)
                    if after is not None:
                        after(j, f)
            each_slab(pe, name, body, peel if after is None else st.slabs)

        def product_part(pe, name, n, xhi, xlo):
            tile, quarter = n // 4, n % 4
            T, j = RING[name] + tile, tile // 2
            par = slab_place(name, j)[1]
            if quarter == 0:
                pe.wait_ge(slab_lo, STAGES[name].first + j + 1)
                pe.wait_ge(tile_free[T % 2], T // 2)
            wh = whi[par][:, :].rearrange("p (k c) -> p k c", k=8)
            wl = wlo[par][:, :].rearrange("p (k c) -> p k c", k=8)
            c = slice(tile % 2 * P, (tile % 2 + 1) * P)
            for k in (2 * quarter, 2 * quarter + 1):
                pe.matmul(psg[:, T % 2, :], wl[:, k, c], xhi[:, k, :], start=(k == 0), stop=False)
                pe.matmul(psg[:, T % 2, :], wh[:, k, c], xlo[:, k, :], start=False, stop=False)
                mm = pe.matmul(psg[:, T % 2, :], wh[:, k, c], xhi[:, k, :], start=False, stop=(k == 7))
            if quarter == 3:
                mm.then_inc(tile_full, 1)

        def part_out(act, name, n, dst):
            if n % 4 == 3:
                tile = n // 4
                T = RING[name] + tile
                act.wait_ge(tile_full, T + 1)
                act.activation(proj2[:, dst(tile), :], psg[:, T % 2, :], ACT.Copy).then_inc(tile_free[T % 2], 1)
                if tile % 2 and tile // 2 + 1 < STAGES[name].slabs:
                    next_hi(act, name, tile // 2 + 1, *slab_place(name, tile // 2 + 1))

        def tokens_by_features(pe, name, xhi, xlo):
            st = STAGES[name]

            def body(j, half, par):
                pe.wait_ge(slab_lo, st.first + j + 1)
                wh = whi[par][:, :].rearrange("p (k c) -> p k c", k=8)
                wl = wlo[par][:, :].rearrange("p (k c) -> p k c", k=8)
                for i in range(NT):
                    b = (RING[name] + i) % 2
                    pe.wait_ge(tile_free[b], half_of(RING[name] + i, st.tiles, j))
                    c = slice(i * P, (i + 1) * P)
                    for k in range(8):
                        pe.matmul(psg[:, b, 0:256], xlo[:, k, c], wh[:, k, :], start=(k == 0), stop=False)
                        pe.matmul(psg[:, b, 0:256], xhi[:, k, c], wl[:, k, :], start=False, stop=False)
                        mm = pe.matmul(psg[:, b, 0:256], xhi[:, k, c], wh[:, k, :], start=False, stop=(k == 7))
                    mm.then_inc(tile_full, 1)
            each_slab(pe, name, body)

        def norm_act(act, n, src, ready, scratch):
            ready(act)
            for i in range(NT):
                act.activation(scratch[:, i, :], src[:, i, :], ACT.Square,
                               accum_out=stat[:, 16 * n + i:16 * n + i + 1]).then_inc(norm_ss, 1)
            act.wait_ge(norm_var, n + 1)
            act.activation(stat[:, 16 * n + 8:16 * n + 12], stat[:, 16 * n + 4:16 * n + 8], ACT.Sqrt).then_inc(norm_sd, 1)

        def norm_dve(dve, n):
            dve.wait_ge(norm_ss, NT * (n + 1))
            dve.tensor_scalar(stat[:, 16 * n + 4:16 * n + 8], stat[:, 16 * n:16 * n + 4], 1.0 / D, EPS,
                              ALU.mult, ALU.add).then_inc(norm_var, 1)
            dve.wait_ge(norm_sd, n + 1)
            dve.reciprocal(stat[:, 16 * n + 12:16 * n + 16], stat[:, 16 * n + 8:16 * n + 12]).then_inc(norm_rs, 1)

        def rstd(n, i):
            return stat[:, 16 * n + 12 + i:16 * n + 13 + i]

        def transposes_of(pe, name, src, made, count):
            pe.wait_ge(made, count)
            for k in range(KD):
                T = RING[name] + k
                if T >= 2:
                    pe.wait_ge(tile_free[T % 2], T // 2)
                for i in range(NT):
                    mm = pe.transpose(psg[:, T % 2, i * P:(i + 1) * P], src[:, i, k * P:(k + 1) * P], ident[:, :])
                mm.then_inc(tile_full, 1)


        def route(dve, link):
            TT, TS = dve.tensor_tensor, dve.tensor_scalar

            def quad(k, a=0, n=NE):
                return rt[:, k, :].rearrange("p (i e) -> p i e", e=NE)[:, :, a:a + n]

            def wide(x, n):
                return x.unsqueeze(2).to_broadcast([P, NT, n])
            T = RING["router_t"]
            dve.wait_ge(tile_full, T + 1)
            bias = rbias[:, :].unsqueeze(1).to_broadcast([P, NT, 36])
            ps = psg[:, T % 2, 0:144].rearrange("p (i c) -> p i c", c=36)
            link(TT(quad(4), ps[:, :, 4:36], bias[:, :, 4:36], ALU.add))
            glog = rt[:, 13, 0:16].rearrange("p (i c) -> p i c", c=4)
            link(TT(glog, ps[:, :, 0:4], bias[:, :, 0:4], ALU.add))
            dve.sem_inc(tile_free[T % 2], 1)
            dve.sem_inc(logits_made, 1)
            small = rt[:, 14, :]
            gmax, r, pg = small[:, 0:4], small[:, 4:8], small[:, 8:12]
            link(dve.tensor_reduce(gmax, glog, AX_X, ALU.max))

            def first_of(out, x, m, dsc, scratch, n):
                link(TT(scratch, x, wide(m, n), ALU.is_equal))
                link(TT(scratch, scratch, dsc, ALU.mult))
                link(dve.tensor_reduce(r, scratch, AX_X, ALU.max))
                link(TT(out, dsc, wide(r, n), ALU.is_equal))
            d4 = desc[:, 28:32].unsqueeze(1).to_broadcast([P, NT, 4])
            d32 = desc[:, :].unsqueeze(1).to_broadcast([P, NT, NE])
            ohg = rt[:, 13, 64:80].rearrange("p (i c) -> p i c", c=4)
            gs = rt[:, 13, 80:96].rearrange("p (i c) -> p i c", c=4)
            first_of(ohg, glog, gmax, d4, gs, 4)
            link(TT(glog, glog, wide(gmax, 4), ALU.subtract))
            dve.sem_inc(route_dve, 1)
            link(TS(gs, ohg, -NEG, NEG, ALU.mult, ALU.add))
            em = quad(4).rearrange("p i (g k) -> p i g k", k=EPG)
            for g in range(NG):
                link(TT(em[:, :, g, :], em[:, :, g, :], gs[:, :, g:g + 1].to_broadcast([P, NT, EPG]), ALU.add))
            m1, m2 = small[:, 12:16], small[:, 16:20]
            link(dve.tensor_reduce(m1, quad(4), AX_X, ALU.max))
            first_of(quad(5), quad(4), m1, d32, quad(6), NE)
            link(TS(quad(6), quad(5), 2 * NEG, None, ALU.mult))
            link(TT(quad(4), quad(4), quad(6), ALU.add))
            link(dve.tensor_reduce(m2, quad(4), AX_X, ALU.max))
            first_of(quad(7), quad(4), m2, d32, quad(6), NE)
            link(TT(rt[:, 11, :], rt[:, 5, :], rt[:, 7, :], ALU.add))
            dve.sem_inc(picks_made, 1)
            link(TT(rt[:, 13, 48:52], m2, m1, ALU.subtract))
            dve.sem_inc(route_dve, 1)
            dve.wait_ge(route_act, 1)
            link(dve.tensor_reduce(small[:, 20:24], rt[:, 13, 16:32].rearrange("p (i c) -> p i c", c=4), AX_X, ALU.add))
            link(dve.reciprocal(pg, small[:, 20:24]))
            dve.wait_ge(route_act, 2)
            ex = rt[:, 13, 52:56]
            link(TS(small[:, 24:28], ex, 1.0, None, ALU.add))
            link(dve.reciprocal(small[:, 28:32], small[:, 24:28]))
            w = rt[:, 12, 0:8].rearrange("p (i k) -> p i k", k=2)
            link(TT(w[:, :, 0], small[:, 28:32], pg, ALU.mult))
            link(TT(w[:, :, 1], w[:, :, 0], ex, ALU.mult))
            T = RING["rank"]
            dve.wait_ge(tile_full, T + 1)
            link(dve.tensor_copy(rt[:, 8:10, :], psg[:, T % 2, 0:256].rearrange("p (a b) -> p a b", b=P)))
            dve.sem_inc(tile_free[T % 2], 1)
            rank, tot = quad(8), quad(9)
            for i in range(1, NT):
                link(TT(rank[:, i, :], rank[:, i, :], tot[:, i - 1, :], ALU.add))
                link(TT(tot[:, i, :], tot[:, i, :], tot[:, i - 1, :], ALU.add))
            cnt = tot[:, NT - 1, :]
            inc, start = rt[:, 10, 0:32], rt[:, 10, 32:64]
            link(dve.tensor_tensor_scan(inc, one[:, 0:NE], cnt, 0.0, ALU.mult, ALU.add))
            link(TT(start, inc, cnt, ALU.subtract))
            iota = rt[:, 10, 64:96]
            link(TS(iota, desc[:, :], -1.0, 32.0, ALU.mult, ALU.add))
            startb = start.unsqueeze(1).to_broadcast([P, NT, NE])
            iotab = iota.unsqueeze(1).to_broadcast([P, NT, NE])
            pos = [rt[:, 15, 8 * q:8 * q + 8].rearrange("p (i k) -> p i k", k=2) for q in range(5)]
            for k, oh in enumerate((quad(5), quad(7))):
                for q, x in enumerate((rank, startb, iotab)):
                    link(TT(quad(6), oh, x, ALU.mult))
                    link(dve.tensor_reduce(pos[q][:, :, k], quad(6), AX_X, ALU.add))
            rk, st, ex_ = rt[:, 15, 0:8], rt[:, 15, 8:16], rt[:, 15, 16:24]
            dest, slot_, far = rt[:, 15, 24:32], rt[:, 15, 32:40], rt[:, 15, 40:48]
            link(TT(dest, rk, st, ALU.add))
            link(dve.scalar_tensor_tensor(out=slot_, in0=ex_, scalar=float(BLK), in1=rk, op0=ALU.mult, op1=ALU.add))
            link(TS(far, dest, float(YS_OVER), None, ALU.add))
            link(TT(far, far, slot_, ALU.subtract))
            link(TS(rt[:, 15, 48:56], rk, float(BLK), None, ALU.is_ge))
            link(TT(far, far, rt[:, 15, 48:56], ALU.mult))
            link(TT(slot_, slot_, far, ALU.add))
            link(dve.tensor_copy(idx[:, 0:8], dest))
            link(dve.tensor_copy(idx[:, 8:16], slot_))
            link(dve.tensor_copy(idx[:, 16:48], start))
            ext, oend, obase = rt[:, 10, 96:128], rt[:, 15, 64:96], rt[:, 15, 96:128]
            link(TS(ext, cnt, float(BLK), None, ALU.is_gt))
            for m in range(2, SEQ // BLK):
                link(TS(rt[:, 6, 0:32], cnt, float(BLK * m), None, ALU.is_gt))
                link(TT(ext, ext, rt[:, 6, 0:32], ALU.add))
            link(dve.tensor_tensor_scan(oend, one[:, 0:NE], ext, 0.0, ALU.mult, ALU.add))
            link(dve.tensor_copy(idx[:, 48:49], oend[:, NE - 1:NE]))
            link(TT(obase, ext, oend, ALU.subtract))
            link(TS(obase, obase, float(BLK), float(BLK), ALU.mult, ALU.add))
            link(TT(obase, obase, start, ALU.add))
            jj = iota[:, 0:OVER]
            ov = ovt[:, 0:OVER, :]
            obj, orow, oval = rt[:, 14, 32:32 + OVER], rt[:, 14, 48:48 + OVER], rt[:, 14, 64:64 + OVER]
            link(TT(ov, oend.unsqueeze(1).to_broadcast([P, OVER, NE]), jj.unsqueeze(2).to_broadcast([P, OVER, NE]),
                    ALU.is_le))
            link(dve.tensor_reduce(obj, ov, AX_X, ALU.add))
            link(TT(ov, iota.unsqueeze(1).to_broadcast([P, OVER, NE]), obj.unsqueeze(2).to_broadcast([P, OVER, NE]),
                    ALU.is_equal))
            link(TT(ov, ov, obase.unsqueeze(1).to_broadcast([P, OVER, NE]), ALU.mult))
            link(dve.tensor_reduce(orow, ov, AX_X, ALU.add))
            link(dve.scalar_tensor_tensor(out=orow, in0=jj, scalar=float(BLK), in1=orow, op0=ALU.mult, op1=ALU.add))
            link(TS(oval, obj, float(NE - 1), None, ALU.is_le))
            link(TS(orow, orow, -float(ASSIGN), None, ALU.add))
            link(TT(orow, orow, oval, ALU.mult))
            link(TS(orow, orow, float(ASSIGN), None, ALU.add))
            link(TS(obj, obj, float(NE - 1), None, ALU.min))
            link(dve.tensor_copy(ovi[:, 0:OVER], obj))
            link(dve.tensor_copy(ovi[:, 16:16 + OVER], orow))
            dve.sem_inc(dest_made, 1)

        def icols(i):
            return slice(i * P, (i + 1) * P)

        def heads(x):
            return x.rearrange("p (h c) -> p h c", c=P)

        def over(x, n=P):
            return x.unsqueeze(2).to_broadcast([x.shape[0], x.shape[1], n])

        def read_done(eng, tag):
            eng.wait_ge(seen(tag), USES[tag][2] + 1)

        def tile_read(eng, T):
            eng.wait_ge(tile_free[T % 2], T // 2 + 1)

        SC = 144
        EGCT, BEG, DSC, GLE, SS2, VAR2, SD2, RS2 = (stat[:, SC + 0:SC + 16], stat[:, SC + 16:SC + 32],
                                                    stat[:, SC + 32:SC + 36], stat[:, SC + 36:SC + 44],
                                                    stat[:, SC + 44:SC + 48], stat[:, SC + 48:SC + 52],
                                                    stat[:, SC + 52:SC + 56], stat[:, SC + 56:SC + 60])
        gle = GLE.rearrange("p (h a) -> p h a", a=2)

        def block2_pe(pe):
            mm_ = pe.matmul
            transposes_of(pe, "xn2", xn2, xn2_made, NT)
            for b in range(2):
                pe.wait_ge(tile_free[b], freed(b, RING["xn2"] + 8))
            features_by_tokens(pe, "small2", acthi, actlo)
            features_by_tokens(pe, "in2q", acthi, actlo)
            for n in range(8):
                product_part(pe, "in2n", n, acthi, actlo)
            for k in range(8):
                begin(pe, ("l2", k))
                pe.wait_ge(l2_sq, k + 1)
                mm_(bank(("l2", k)), one[:, :], c4[k % 2][:, :], start=True, stop=True).then_inc(x_full, 1)
            begin(pe, "smalltok")
            pe.wait_ge(rows_made, 3)
            for i in range(NT):
                mm = pe.transpose(bank("smalltok")[:, icols(i)], smallT[:, icols(i)], ident[:, :])
            mm.then_inc(x_full, 1)
            pe.wait_ge(const2_in, 48)
            for i in range(NT):
                gdn_pe(pe, i)
            nsa_pe(pe)
            pe.wait_ge(branch_lo, 1)
            features_by_tokens(pe, "gdn_out", act2hi, act2lo)
            pe.wait_ge(branch_lo, 2)
            features_by_tokens(pe, "nsa_out", act2hi[:, 4:8, :], act2lo[:, 4:8, :])
            pe.wait_ge(merged2_lo, 8)
            tokens_by_features(pe, "out2", acthi, actlo)
            transposes_of(pe, "xnf", xnf, xnf_made, NT)
            for b in range(2):
                pe.wait_ge(tile_free[b], freed(b, RING["xnf"] + 8))
            features_by_tokens(pe, "gate_up", acthi, actlo)
            for b in range(2):
                pe.wait_ge(tile_free[b], freed(b, RING["down"]))
            acc = [psg[:, 0, :], psg[:, 1, :]] + [psx[:, b, :] for b in range(6)]
            first = STAGES["down"].first

            def down_slab(j, par, start=False, stop=False):
                pe.wait_ge(slab_lo, first + j + 1)
                wh = whi[par][:, :].rearrange("p (k c) -> p k c", k=2)
                wl = wlo[par][:, :].rearrange("p (k c) -> p k c", k=2)
                pe.wait_ge(h_lo, 2 * j + 2)
                for kk in range(2):
                    xh = hhi[:, bass.ds(2 * j + kk, 1), :].rearrange("p a c -> p (a c)")
                    xl = hlo[:, bass.ds(2 * j + kk, 1), :].rearrange("p a c -> p (a c)")
                    for d in range(8):
                        c = slice(d * P, (d + 1) * P)
                        pe.matmul(acc[d], wl[:, kk, c], xh, start=start and kk == 0, stop=False)
                        pe.matmul(acc[d], wh[:, kk, c], xl, start=False, stop=False)
                        mm = pe.matmul(acc[d], wh[:, kk, c], xh, start=False, stop=stop and kk == 1)
                mm.then_inc(down_used, 1)
            down_slab(0, first % 2, start=True)
            with pe.Fori(0, 4) as i:
                for u in range(1, 3):
                    down_slab(2 * i + u, (first + u) % 2)
            down_slab(9, (first + 9) % 2)
            down_slab(10, (first + 10) % 2, stop=True)
            pe.wait_ge(outT_made, 8)
            for i in range(NT):
                for h in range(2):
                    T = RING["outT"] + 2 * i + h
                    pe.wait_ge(tile_free[T % 2], T // 2)
                    for d in range(4):
                        mm = pe.transpose(psg[:, T % 2, d * P:(d + 1) * P], outT[:, 4 * h + d, icols(i)], ident[:, :])
                    mm.then_inc(tile_full, 1)

        def gdn_part(i, l):
            return 8 + 8 * i + 2 * (l - 1)

        def nsa_parts(n):
            return range(n + (n + 2) // 3, n + 1 + (n + 3) // 3)

        def gate_slot(f):
            return f if f < 8 else (f + 4 if f < 13 else f + 8)

        def gates2(f):
            return proj2[:, gate_slot(f), :]

        def gdn_pe(pe, i):
            mm_ = pe.matmul
            c = icols(i)
            hb = [slice(h * P, (h + 1) * P) for h in range(GH)]
            begin(pe, ("gc", i))
            for h in range(GH):
                mm = mm_(bank(("gc", i))[:, hb[h]], sel[32:36, h, :], smallT[32:36, c], start=True, stop=True)
            mm.then_inc(x_full, 1)
            begin(pe, ("beta", i))
            for h in range(GH):
                mm = mm_(bank(("beta", i))[:, hb[h]], sel[0:4, h, :], smallT[0:4, c], start=True, stop=True)
            mm.then_inc(x_full, 1)
            if i == 0:
                pe.wait_ge(l2_made, 8)
                pe.wait_ge(values_made, 1)
            for tag, slot0 in ((("ktok", i), 4), (("vtok", i), 8)):
                begin(pe, tag)
                for h in range(GH):
                    mm = pe.transpose(bank(tag)[:, hb[h]], proj2[:, slot0 + h, c], ident[:, :])
                mm.then_inc(x_full, 1)
            begin(pe, ("AT", i))
            read_done(pe, ("beta", i))
            for h in range(GH):
                mm = mm_(bank(("AT", i))[:, hb[h]], proj2[:, 4 + h, c], kbT[:, h, :], start=True, stop=True)
            mm.then_inc(x_full, 1)
            begin(pe, ("QK", i))
            for h in range(GH):
                mm = mm_(bank(("QK", i))[:, hb[h]], proj2[:, 4 + h, c], proj2[:, h, c], start=True, stop=True)
            mm.then_inc(x_full, 1)
            begin(pe, ("D0", i))
            pe.wait_ge(Q["DT0"], i + 1)
            for h in range(GH):
                mm = pe.transpose(bank(("D0", i))[:, hb[h]], DT[:, h, :], ident[:, :])
            mm.then_inc(x_full, 1)
            for l in range(1, LEVELS):
                begin(pe, ("P1", i, l))
                pe.wait_ge(gdn_pool, (LEVELS - 1) * i + l)
                if l == 1:
                    read_done(pe, ("D0", i))
                else:
                    read_done(pe, ("P2", i, l - 1))
                for h in range(GH):
                    mm = mm_(bank(("P1", i, l))[:, hb[h]], AL[l % 2][:, h, :], Dm[:, h, :], start=True, stop=True)
                mm.then_inc(x_full, 1)
                if l < LEVELS - 1:
                    product_part(pe, "in2n", gdn_part(i, l), acthi, actlo)
                read_done(pe, ("P1", i, l))
                if l > 1:
                    read_done(pe, ("P3", i, l - 1))
                if l < LEVELS - 1:
                    begin(pe, ("P2", i, l))
                    for h in range(GH):
                        mm = mm_(bank(("P2", i, l))[:, hb[h]], DT[:, h, :], P1s[:, h, :], start=True, stop=True)
                    mm.then_inc(x_full, 1)
                begin(pe, ("P3", i, l))
                for h in range(GH):
                    mm = mm_(bank(("P3", i, l))[:, hb[h]], P1s[:, h, :], DT[:, h, :], start=True, stop=True)
                mm.then_inc(x_full, 1)
                if l < LEVELS - 1:
                    product_part(pe, "in2n", gdn_part(i, l) + 1, acthi, actlo)
            begin(pe, ("wT", i))
            read_done(pe, ("P3", i, LEVELS - 1))
            pe.wait_ge(Q["scaled"], 3 * i + 3)
            for h in range(GH):
                mm = mm_(bank(("wT", i))[:, hb[h]], kbg[:, h, :], DT[:, h, :], start=True, stop=True)
            mm.then_inc(x_full, 1)
            begin(pe, ("u", i))
            for h in range(GH):
                mm = mm_(bank(("u", i))[:, hb[h]], DT[:, h, :], vb[:, h, :], start=True, stop=True)
            mm.then_inc(x_full, 1)
            for a in range(2):
                r = slice(CHUNK * a, CHUNK * a + CHUNK)
                begin(pe, ("V", i, a))
                if a == 0:
                    read_done(pe, ("wT", i))
                pe.wait_ge(Q["S"], 2 * i + a + 1)
                for h in range(GH):
                    mm = mm_(bank(("V", i, a))[r, hb[h]], nwT[:, h, r], S[:, h, :], start=True, stop=True)
                mm.then_inc(x_full, 1)
                if a == 0:
                    begin(pe, ("O", i))
                    pe.wait_ge(Q["qgT"], i + 1)
                    pe.wait_ge(Q["masked"], 2 * i + 2)
                pe.wait_ge(Q["vn"], 2 * i + a + 1)
                for h in range(GH):
                    mm_(bank(("O", i))[r, hb[h]], qgT[:, h, r], S[:, h, :], start=True, stop=False)
                    mm = mm_(bank(("O", i))[r, hb[h]], qkT[r, h, r], vn[r, h, :], start=False, stop=True)
                if a == 1:
                    mm.then_inc(x_full, 1)
                begin(pe, ("S", i, a))
                for h in range(GH):
                    mm = mm_(bank(("S", i, a))[:, hb[h]], kd[r, h, :], vn[r, h, :], start=True, stop=True)
                mm.then_inc(x_full, 1)
            begin(pe, ("oT", i))
            pe.wait_ge(Q["on"], i + 1)
            for h in range(GH):
                mm = pe.transpose(bank(("oT", i))[:, hb[h]], on[:, h, :], ident[:, :])
            mm.then_inc(x_full, 1)

        ROPED = (17, 18, 19, 20, 21, 23, 25)

        def keys_of(br, i):
            return 31 if br == 0 else (i + 1) * P

        def nsa_pe(pe):
            mm_ = pe.matmul
            pe.wait_ge(const3_in, 160)
            for k, s_ in enumerate(ROPED):
                begin(pe, ("rope", k))
                mm_(bank(("rope", k)), rotp[:, :], proj2[:, s_, :], start=True, stop=True).then_inc(x_full, 1)
            for tag, s_ in (("vslc", 24), ("vwin", 26)):
                begin(pe, tag)
                for i in range(NT):
                    mm = pe.transpose(bank(tag)[:, icols(i)], proj2[:, s_, icols(i)], ident[:, :])
                mm.then_inc(x_full, 1)
            for b, tag in enumerate(("hidk", "hidv")):
                begin(pe, tag)
                pe.wait_ge(Q2["blk"], 8 * b + 8)
                for a in range(16):
                    mm = mm_(bank(tag)[:, 0:62], w1[b][:, a, :], blk[b][:, a, :], start=(a == 0), stop=(a == 15))
                mm.then_inc(x_full, 1)
            begin(pe, "kc")
            read_done(pe, "hidk")
            mm_(bank("kc")[:, 0:62], w2s[:, 0:128], hid[:, 0, :], start=True, stop=True).then_inc(x_full, 1)
            begin(pe, "vc")
            read_done(pe, "hidv")
            for g in range(2):
                mm = mm_(bank("vc")[0:31, 64 * g:64 * g + 64], hid[:, 1, 31 * g:31 * g + 31], w2s[:, 128:192],
                         start=True, stop=True)
            mm.then_inc(x_full, 1)

            def scores2(n):
                i, g, hp, br = STEPS[n]
                W = keys_of(br, i)
                for par, tag in enumerate((("sc", n), ("sc2", n))):
                    r = slice(64 * par, 64 * par + 64)
                    begin(pe, tag)
                    k = (kcd, kds, kdw)[br][r, g, 0:W]
                    mm_(bank(tag)[:, 0:W], proj2[r, 17 + 2 * g + hp, icols(i)], k, start=True, stop=True).then_inc(x_full, 1)

            pe.wait_ge(Q2["keys"], 8)
            read_done(pe, "kc")
            read_done(pe, "vc")
            read_done(pe, "vslc")
            read_done(pe, "vwin")
            scores2(0)
            scores2(1)
            for n, (i, g, hp, br) in enumerate(STEPS):
                pe.wait_ge(scale_made, n + 1)
                cs = chunks_T(i, br)
                for ci, tiles in enumerate(cs):
                    tag = ("pT", n, ci)
                    begin(pe, tag)
                    for jj, j in enumerate(tiles):
                        for par in range(2):
                            o = slice((2 * jj + par) * P, (2 * jj + par + 1) * P)
                            if br == 0:
                                mm = mm_(bank(tag)[0:31, o], pr[n % 2][:, par, 0:31], scale[n % 2][:, par, :],
                                         start=True, stop=True)
                            else:
                                mm = mm_(bank(tag)[:, o], pr[n % 2][:, par, icols(j)], scale[n % 2][:, par, :],
                                         start=True, stop=True)
                    mm.then_inc(x_full, 1)
                    if ci == 0:
                        if n + 2 < len(STEPS):
                            scores2(n + 2)
                        for part in nsa_parts(n):
                            product_part(pe, "in2m", part, acthi, actlo)
                read_done(pe, ("pT", n, len(cs) - 1))
                if hp == 0 and br == 0:
                    begin(pe, ("o", i, g))
                o = bank(("o", i, g))[0:64, 256 * hp:256 * hp + 256]
                tiles = [0] if br == 0 else range(i + 1)
                for j in tiles:
                    if br == 0:
                        v, p_ = vct[0:31, g, :], prT[n % 2][0:31, 0, :, :]
                    else:
                        v, p_ = (vtS, vtW)[br - 1][:, j, 64 * g:64 * g + 64], prT[n % 2][:, j, :, :]
                    mm = mm_(o, v, p_, start=(br == 0), stop=(br == 2 and j == i))
                if hp == 1 and br == 2:
                    mm.then_inc(x_full, 1)

        def block2_act(act, link):
            A = act.activation
            norm_act(act, 2, hres, lambda e: e.wait_ge(combined, 2 * NT), xn2)
            norm_act(act, 3, hres, lambda e: e.wait_ge(final1_made, NT), xn2)
            upper_tiles(act, "xn2", "mix_gain", xn2_hi)
            T = RING["small2"]
            each_slab_act(act, "small2", lambda j, half, par: None)
            act.wait_ge(tile_full, T + 1)
            A(smallT, psg[:, T % 2, :], ACT.Copy).then_inc(tile_free[T % 2], 1)
            tile_read(act, T)
            A(smallT[0:4, :], smallT[0:4, :], ACT.Sigmoid).then_inc(rows_made, 1)
            A(smallT[64:88, :], smallT[64:88, :], ACT.Sigmoid).then_inc(rows_made, 1)
            a0 = VEC["a_log"][0]
            A(stat[32:36, 141:142], vec[32:36, a0:a0 + 1], ACT.Exp).then_inc(small_act, 1)
            act.wait_ge(small_dve, 1)
            link(A(rowt[1][32:36, :], rowt[1][32:36, :], ACT.Exp, scale=-1.0))
            A(rowt[1][32:36, :], rowt[1][32:36, :], ACT.Ln, bias=one[32:36, 0:1]).then_inc(small_act, 1)
            evacuate(act, "in2q", proj2, 1, ACT.Copy)
            act.wait_ge(conv2_made, 32)
            link(A(proj2[:, 0:8, :], proj2[:, 0:8, :], ACT.Silu))
            next_hi(act, "in2n", 0, *slab_place("in2n", 0))
            for n in range(8):
                part_out(act, "in2n", n, attention_slot)
            for k in range(8):
                if k >= 2:
                    filled(act, ("l2", k - 2))
                A(c4[k % 2][:, :], proj2[:, k, :], ACT.Square).then_inc(l2_sq, 1)
                filled(act, ("l2", k))
                if k >= 2:
                    act.wait_ge(l2_made, k - 1)
                A(l2r[k % 2][:, :], bank(("l2", k)), ACT.Sqrt, bias=stat[:, 140:141]).then_inc(seen(("l2", k)), 1)
            act.wait_ge(conv2_made, 48)
            for b in range(2):
                act.wait_ge(tile_free[b], freed(b, RING["in2n"]))
            A(proj2[:, 8:12, :], proj2[:, 8:12, :], ACT.Silu).then_inc(values_made, 1)
            A(proj2[:, 13:17, :], proj2[:, 13:17, :], ACT.Silu).then_inc(values_made, 1)
            read_done(act, "smalltok")
            A(EGCT.rearrange("p (i h) -> p i h", h=4), smalltok[:, :, 32:36], ACT.Exp).then_inc(small_act, 1)
            for i in range(NT):
                gdn_act_tile(act, i)
            nsa_act(act)
            act.wait_ge(nsa_done, 1)
            A(act2hi[:, 0:4, :], proj2[:, 8:12, :], ACT.Copy).then_inc(branch_hi, 1)
            A(act2hi[:, 4:8, :], proj2[:, 17:21, :], ACT.Copy).then_inc(branch_hi, 1)
            for b in range(2):
                act.wait_ge(tile_free[b], freed(b, RING["gdn_out"]))
            for a, b in ((0, 8), (12, 17), (21, 24)):
                A(proj2[:, a:b, :], proj2[:, a:b, :], ACT.Sigmoid).then_inc(gates2_made, 1)
            each_slab_act(act, "gdn_out", lambda j, half, par: None)

            def merged_upper(j, half, par):
                for f in range(4):
                    act.wait_ge(merged2_made, 4 * j + f + 1)
                    A(acthi[:, 4 * j + f, :], gates2(4 * j + f), ACT.Copy).then_inc(merged2_hi, 1)
            each_slab_act(act, "nsa_out", merged_upper)
            each_slab_act(act, "out2", lambda j, half, par: None)
            norm_act(act, 4, hres, lambda e: e.wait_ge(x3_made, 1), xnf)
            upper_tiles(act, "xnf", "ffn_gain", xnf_hi)

            def gated(j, half, par):
                T = RING["gate_up"]
                b = par
                act.wait_ge(tile_full, T + 2 * j + 1)
                if not isinstance(j, int) or j >= 2:
                    act.wait_ge(h_made, j - 1)
                A(sgb[b][:, :], psg[:, T % 2, :], ACT.Silu).then_inc(tile_free[T % 2], 1)
                act.wait_ge(h_made, j + 1)
                A(hhi[:, bass.ds(j, 1), :].rearrange("p a c -> p (a c)"), hv[b][:, :], ACT.Copy).then_inc(h_hi, 1)
            each_slab_act(act, "gate_up", gated, 2)
            first = STAGES["down"].first

            def down_hi(j, used, half, par):
                if used is None:
                    act.wait_ge(tile_full, RING["down"])
                else:
                    act.wait_ge(down_used, used)
                act.wait_ge(slab_loaded[par], 32 * half + 32)
                A(whi[par][:, :], raw[par][:, :], ACT.Copy).then_inc(slab_hi, 1)
            down_hi(1, None, (first + 1) // 2, (first + 1) % 2)
            with act.Fori(0, 4) as i:
                for u in range(2, 4):
                    down_hi(2 * i + u, 2 * i + u - 1, i + (first + u) // 2, (first + u) % 2)
            down_hi(10, 9, (first + 10) // 2, (first + 10) % 2)
            act.wait_ge(down_used, 11)
            acc = [psg[:, 0, :], psg[:, 1, :]] + [psx[:, b, :] for b in range(6)]
            for d in range(4):
                A(outT[:, d, :], acc[d], ACT.Copy).then_inc(outT_made, 1)
            norm_act(act, 5, hres, lambda e: e.wait_ge(x4_made, 1), fscr)

        def upper_tiles(act, name, gain, made):
            for k in range(KD):
                T = RING[name] + k
                act.wait_ge(tile_full, T + 1)
                act.activation(acthi[:, k, :], psg[:, T % 2, :], ACT.Copy, scale=vc(gain, k)).then_inc(made, 1)

        def lower_tiles(dve, name, gain, made):
            for k in range(KD):
                T = RING[name] + k
                dve.wait_ge(made, k + 1)
                dve.scalar_tensor_tensor(out=actlo[:, k, :], in0=psg[:, T % 2, :], scalar=vc(gain, k),
                                         in1=acthi[:, k, :].bitcast(F32), op0=ALU.mult, op1=ALU.subtract)\
                   .then_inc(tile_free[T % 2], 1)

        def evacuate(act, name, dst, slot0, func):
            def body(j, half, par):
                for f in range(2):
                    T = RING[name] + f
                    act.wait_ge(tile_full, T + 2 * j + 1)
                    act.activation(dst[:, bass.ds(slot0 + 2 * j + f, 1), :].rearrange("p a c -> p (a c)"),
                                   psg[:, T % 2, :], func).then_inc(tile_free[T % 2], 1)
            each_slab_act(act, name, body)

        def attention_slot(f):
            return 17 + f

        def gdn_act_tile(act, i):
            A = act.activation
            filled(act, ("gc", i))
            A(gcb[:, :, :], heads(bank(("gc", i))), ACT.Copy).then_inc(seen(("gc", i)), 1)
            read_done(act, ("gc", i))
            A(egc[:, :, :], gcb[:, :, :], ACT.Exp).then_inc(Q["egc"], 1)
            A(gle, gcb[:, :, CHUNK - 1:P:CHUNK], ACT.Exp).then_inc(Q["gle"], 1)
            filled(act, ("ktok", i))
            A(ktok[:, :, :], heads(bank(("ktok", i))), ACT.Copy).then_inc(seen(("ktok", i)), 1)
            act.wait_ge(Q["dsc_in"], 2 * i + 2)
            A(DSC, DSC, ACT.Exp).then_inc(Q["dsc"], 1)
            act.wait_ge(Q["dec_in"], 4 * i + 4)
            A(decS[:, :, :], decS[:, :, :], ACT.Exp).then_inc(Q["dec"], 1)
            filled(act, ("D0", i))
            A(Dm[:, :, :], heads(bank(("D0", i))), ACT.Copy).then_inc(seen(("D0", i)), 1)
            for l in range(1, LEVELS):
                filled(act, ("P1", i, l))
                A(P1s[:, :, :], heads(bank(("P1", i, l))), ACT.Copy).then_inc(seen(("P1", i, l)), 1)
                if l > 1:
                    for n in range(2):
                        part_out(act, "in2n", gdn_part(i, l - 1) + n, attention_slot)
            filled(act, ("wT", i))
            A(nwT[:, :, :], heads(bank(("wT", i))), ACT.Copy, scale=-1.0).then_inc(seen(("wT", i)), 1)
            filled(act, ("u", i))
            A(u_[:, :, :], heads(bank(("u", i))), ACT.Copy).then_inc(seen(("u", i)), 1)
            filled(act, ("O", i))
            act.wait_ge(Q["S"], 2 * i + 3)
            for h in range(GH):
                A(Sg[:, h, :], bank(("O", i))[:, h * P:(h + 1) * P], ACT.Square,
                  accum_out=SS2[:, h:h + 1]).then_inc(Q["sq"], 1)
            act.wait_ge(Q["var"], i + 1)
            A(SD2, VAR2, ACT.Sqrt).then_inc(Q["sd"], 1)

        def nsa_act(act):
            A = act.activation
            for tag, dst in (("vslc", vtS), ("vwin", vtW)):
                filled(act, tag)
                A(dst[:, :, :], heads(bank(tag)), ACT.Copy).then_inc(seen(tag), 1)
            for b, tag in enumerate(("hidk", "hidv")):
                filled(act, tag)
                A(hid[:, b, :], bank(tag)[:, 0:62], ACT.Silu).then_inc(seen(tag), 1)
            filled(act, "kc")
            A(kcd[:, :, :], bank("kc")[:, 0:62].rearrange("p (g n) -> p g n", n=31), ACT.Copy, scale=0.125)\
                .then_inc(seen("kc"), 1)
            filled(act, "vc")
            A(vct[0:31, :, :], bank("vc")[0:31, 0:128].rearrange("p (g d) -> p g d", d=64), ACT.Copy)\
                .then_inc(seen("vc"), 1)

            def exps(n):
                i, g, hp, br = STEPS[n]
                W = keys_of(br, i)
                b = n % 2
                act.wait_ge(sm_max, n + 1)
                for par, tag in enumerate((("sc", n), ("sc2", n))):
                    A(pr[b][:, par, 0:W], bank(tag)[:, 0:W], ACT.Exp, bias=stat[:, 220 + 2 * b + par:221 + 2 * b + par],
                      accum_out=stat[:, 224 + 2 * b + par:225 + 2 * b + par]).then_inc(seen(tag), 1)
            next_hi(act, "in2m", 0, *slab_place("in2m", 0))
            exps(0)
            exps(1)
            for n, (i, g, hp, br) in enumerate(STEPS):
                for ci, tiles in enumerate(chunks_T(i, br)):
                    tag = ("pT", n, ci)
                    filled(act, tag)
                    if br == 0:
                        A(prT[n % 2][0:31, 0, :, :], bank(tag)[0:31, 0:256].rearrange("p (a c) -> p a c", c=P), ACT.Copy)\
                            .then_inc(seen(tag), 1)
                    else:
                        m = len(tiles)
                        A(prT[n % 2][:, tiles[0]:tiles[0] + m, :, :],
                          bank(tag)[:, 0:256 * m].rearrange("p (j a c) -> p j a c", a=2, c=P), ACT.Copy)\
                            .then_inc(seen(tag), 1)
                if n + 2 < len(STEPS):
                    exps(n + 2)
                if n > 0:
                    for part in nsa_parts(n - 1):
                        part_out(act, "in2m", part, gate_slot)
            for part in nsa_parts(len(STEPS) - 1):
                part_out(act, "in2m", part, gate_slot)

        def block2_dve(dve, link):
            TT, TS, STT = dve.tensor_tensor, dve.tensor_scalar, dve.scalar_tensor_tensor
            norm_dve(dve, 2)
            dve.wait_ge(norm_rs, 3)
            dve.wait_ge(gf_in, 16)
            for i in range(NT):
                STT(out=hres[:, i, :], in0=hres[:, i, :], scalar=rstd(2, i), in1=gfb[:, :], op0=ALU.mult,
                    op1=ALU.mult).then_inc(final1_made, 1)
            norm_dve(dve, 3)
            dve.wait_ge(norm_rs, 4)
            for i in range(NT):
                TS(xn2[:, i, :], hres[:, i, :], rstd(3, i), None, ALU.mult).then_inc(xn2_made, 1)
            lower_tiles(dve, "xn2", "mix_gain", xn2_hi)
            tile_read(dve, RING["small2"])
            d0 = VEC["dt_bias"][0]
            r = slice(32, 36)
            link(TS(rowt[0][r, :], smallT[r, :], vec[r, d0:d0 + 1], None, ALU.add))
            link(STT(out=rowt[1][r, :], in0=rowt[0][r, :], scalar=-1.0, in1=rowt[0][r, :], op0=ALU.mult, op1=ALU.max))
            dve.sem_inc(small_dve, 1)
            dve.wait_ge(small_act, 2)
            link(STT(out=rowt[0][r, :], in0=rowt[0][r, :], scalar=0.0, in1=rowt[1][r, :], op0=ALU.max, op1=ALU.add))
            link(TS(rowt[0][r, :], rowt[0][r, :], stat[r, 141:142], -1.0, ALU.mult, ALU.mult))
            dve.wait_ge(const2_in, 48)
            dve.tensor_tensor_scan(smallT[r, :], cgo[r, :], rowt[0][r, :], 0.0, ALU.mult, ALU.add).then_inc(rows_made, 1)
            for f in range(12):
                tile_read(dve, RING["in2q"] + f)
                w = [vc("conv2", 4 * f + j) for j in range(4)]
                x, y = proj2[:, 1 + f, :], proj2[:, f, :]
                if f:
                    dve.wait_ge(conv2_made, 4 * f)
                TS(y, x, w[3], None, ALU.mult).then_inc(conv2_made, 1)
                for s_ in range(1, 4):
                    dve.wait_ge(conv2_made, 4 * f + s_)
                    STT(out=y[:, s_:SEQ], in0=x[:, 0:SEQ - s_], scalar=w[3 - s_], in1=y[:, s_:SEQ], op0=ALU.mult,
                        op1=ALU.add).then_inc(conv2_made, 1)
            for k in range(8):
                read_done(dve, ("l2", k))
                link(dve.reciprocal(l2r[k % 2][:, :], l2r[k % 2][:, :]))
                STT(out=proj2[:, k, :], in0=proj2[:, k, :], scalar=(128.0 ** -0.5 if k < 4 else 1.0),
                    in1=l2r[k % 2][:, :], op0=ALU.mult, op1=ALU.mult).then_inc(l2_made, 1)
            filled(dve, "smalltok")
            dve.tensor_copy(smalltok, heads(bank("smalltok"))).then_inc(seen("smalltok"), 1)
            read_done(dve, "smalltok")
            dve.wait_ge(small_act, 3)
            link(TT(BEG.rearrange("p (i h) -> p i h", h=4), EGCT.rearrange("p (i h) -> p i h", h=4), smalltok[:, :, 0:4],
                    ALU.mult))
            dve.memset(S[:, :, :], 0.0).then_inc(Q["S"], 1)
            for i in range(NT):
                gdn_dve_tile(dve, link, i)
            nsa_dve_(dve, link)
            dve.wait_ge(branch_hi, 1)
            TT(act2lo[:, 0:4, :], proj2[:, 8:12, :], act2hi[:, 0:4, :].bitcast(F32), ALU.subtract).then_inc(branch_lo, 1)
            dve.wait_ge(branch_hi, 2)
            TT(act2lo[:, 4:8, :], proj2[:, 17:21, :], act2hi[:, 4:8, :].bitcast(F32), ALU.subtract).then_inc(branch_lo, 1)
            dve.wait_ge(gates2_made, 3)
            for f in range(8):
                T = RING["gdn_out"] + f
                dve.wait_ge(tile_full, T + 1)
                TT(gates2(f), psg[:, T % 2, :], gates2(f), ALU.mult).then_inc(tile_free[T % 2], 1)
            for f in range(8):
                T = RING["nsa_out"] + f
                dve.wait_ge(tile_full, T + 1)
                TT(gates2(8 + f), psg[:, T % 2, :], gates2(8 + f), ALU.mult).then_inc(tile_free[T % 2], 1)
                tile_read(dve, T)
                TT(gates2(f), gates2(f), gates2(8 + f), ALU.add).then_inc(merged2_made, 1)
                dve.wait_ge(merged2_hi, f + 1)
                TT(actlo[:, f, :], gates2(f), acthi[:, f, :].bitcast(F32), ALU.subtract).then_inc(merged2_lo, 1)
            add_product(dve, "out2")
            for b in range(2):
                dve.wait_ge(tile_free[b], freed(b, RING["out2"] + 16))
            dve.sem_inc(x3_made, 1)
            norm_dve(dve, 4)
            dve.wait_ge(norm_rs, 5)
            for i in range(NT):
                TS(xnf[:, i, :], hres[:, i, :], rstd(4, i), None, ALU.mult).then_inc(xnf_made, 1)
            lower_tiles(dve, "xnf", "ffn_gain", xnf_hi)

            def hidden(j, half, par):
                T = RING["gate_up"]
                b = par
                dve.wait_ge(tile_full, T + 2 * j + 2)
                dve.wait_ge(tile_free[T % 2], T // 2 + 1 + j)
                if not isinstance(j, int) or j >= 2:
                    dve.wait_ge(h_lo, j - 1)
                TT(hv[b][:, :], psg[:, 1 - T % 2, :], sgb[b][:, :], ALU.mult).then_inc(h_made, 1)
                dve.wait_ge(h_made, j + 1)
                dve.sem_inc(tile_free[1 - T % 2], 1)
                dve.wait_ge(h_hi, j + 1)
                TT(hlo[:, bass.ds(j, 1), :].rearrange("p a c -> p (a c)"), hv[b][:, :],
                   hhi[:, bass.ds(j, 1), :].rearrange("p a c -> p (a c)").bitcast(F32), ALU.subtract).then_inc(h_lo, 1)
            each_slab(dve, "gate_up", hidden, 2)
            dve.wait_ge(down_used, 11)
            acc = [psg[:, 0, :], psg[:, 1, :]] + [psx[:, b, :] for b in range(6)]
            for d in range(4, 8):
                dve.tensor_copy(outT[:, d, :], acc[d]).then_inc(outT_made, 1)
            for i in range(NT):
                for h in range(2):
                    T = RING["outT"] + 2 * i + h
                    dve.wait_ge(tile_full, T + 1)
                    dst = hres[:, i, 512 * h:512 * h + 512]
                    TT(dst, dst, psg[:, T % 2, :], ALU.add).then_inc(tile_free[T % 2], 1)
            for b in range(2):
                dve.wait_ge(tile_free[b], freed(b, RING["outT"] + 8))
            dve.sem_inc(x4_made, 1)
            norm_dve(dve, 5)
            dve.wait_ge(norm_rs, 6)
            dve.wait_ge(gout_in, 16)
            for i in range(NT):
                STT(out=fin[:, i, :], in0=hres[:, i, :], scalar=rstd(5, i), in1=goutb[:, :], op0=ALU.mult,
                    op1=ALU.mult).then_inc(out_made, 1)

        def add_product(dve, name):
            def body(j, half, par):
                for i in range(NT):
                    T = RING[name] + i
                    dve.wait_ge(tile_full, T + 4 * j + 1)
                    dst = hres[:, i, bass.ds(256 * j, 256)]
                    dve.tensor_tensor(dst, dst, psg[:, T % 2, 0:256], ALU.add).then_inc(tile_free[T % 2], 1)
            each_slab(dve, name, body)

        def gdn_dve_tile(dve, link, i):
            TT, TS, STT = dve.tensor_tensor, dve.tensor_scalar, dve.scalar_tensor_tensor
            c = icols(i)
            gct, bt = smalltok[:, i, 32:36], smalltok[:, i, 0:4]
            filled(dve, ("beta", i))
            TT(kbT[:, :, :], proj2[:, 4:8, c], heads(bank(("beta", i))), ALU.mult).then_inc(seen(("beta", i)), 1)
            read_done(dve, ("gc", i))
            for a in range(2):
                r = slice(CHUNK * a, CHUNK * a + CHUNK)
                TT(DSC[r, :], gcb[r, :, CHUNK * a + CHUNK - 1], gct[r, :], ALU.subtract).then_inc(Q["dsc_in"], 1)
            for h in range(GH):
                TS(decS[:, h, :], gcb[:, h, :], gct[:, h:h + 1], 0.0, ALU.subtract, ALU.min).then_inc(Q["dec_in"], 1)
            dve.wait_ge(Q["egc"], i + 1)
            TT(qgT[:, :, :], proj2[:, 0:4, c], egc[:, :, :], ALU.mult).then_inc(Q["qgT"], 1)
            filled(dve, ("vtok", i))
            TT(vb[:, :, :], heads(bank(("vtok", i))), over(bt), ALU.mult).then_inc(seen(("vtok", i)), 1)
            read_done(dve, ("vtok", i))
            dve.sem_inc(Q["scaled"], 1)
            read_done(dve, ("ktok", i))
            TT(kbg[:, :, :], ktok[:, :, :], over(BEG[:, 4 * i:4 * i + 4]), ALU.mult).then_inc(Q["scaled"], 1)
            dve.wait_ge(Q["dsc"], i + 1)
            TT(kd[:, :, :], ktok[:, :, :], over(DSC), ALU.mult).then_inc(Q["scaled"], 1)
            dve.wait_ge(Q["dec"], i + 1)
            link(TT(decI[:, :, :], decS[:, :, :], gm(1), ALU.mult))
            link(TT(decS[:, :, :], decS[:, :, :], gm(0), ALU.mult))
            filled(dve, ("AT", i))
            TT(AT[:, :, :], heads(bank(("AT", i))), decS[:, :, :], ALU.mult).then_inc(seen(("AT", i)), 1)
            read_done(dve, ("AT", i))
            dve.sem_inc(gdn_at, 1)
            dve.sem_inc(Q["masked"], 1)
            link(TT(Dm[:, :, :], AT[:, :, :], gm(2), ALU.mult))
            TT(DT[:, :, :], ident[:, :].unsqueeze(1).to_broadcast([P, GH, P]), Dm[:, :, :], ALU.subtract)\
                .then_inc(Q["DT0"], 1)
            filled(dve, ("QK", i))
            TT(qkT[:, :, :], heads(bank(("QK", i))), decI[:, :, :], ALU.mult).then_inc(seen(("QK", i)), 1)
            read_done(dve, ("QK", i))
            dve.sem_inc(Q["masked"], 1)
            read_done(dve, ("D0", i))
            for l in range(1, LEVELS):
                if l < LEVELS - 1:
                    filled(dve, ("P2", i, l))
                    TT(Dm[:, :, :], Dm[:, :, :], heads(bank(("P2", i, l))), ALU.subtract).then_inc(seen(("P2", i, l)), 1)
                    read_done(dve, ("P2", i, l))
                filled(dve, ("P3", i, l))
                TT(DT[:, :, :], DT[:, :, :], heads(bank(("P3", i, l))), ALU.subtract).then_inc(seen(("P3", i, l)), 1)
                read_done(dve, ("P3", i, l))
            dve.wait_ge(Q["gle"], i + 1)
            read_done(dve, ("u", i))
            for a in range(2):
                r = slice(CHUNK * a, CHUNK * a + CHUNK)
                filled(dve, ("V", i, a))
                TT(vn[r, :, :], u_[r, :, :], heads(bank(("V", i, a))[r, :]), ALU.add).then_inc(seen(("V", i, a)), 1)
                read_done(dve, ("V", i, a))
                dve.sem_inc(Q["vn"], 1)
                if a == 0 and i > 0:
                    dve.wait_ge(Q["sq"], 4 * i)
                link(TT(Sg[:, :, :], S[:, :, :], over(gle[:, :, a]), ALU.mult))
                filled(dve, ("S", i, a))
                TT(S[:, :, :], Sg[:, :, :], heads(bank(("S", i, a))), ALU.add).then_inc(seen(("S", i, a)), 1)
                read_done(dve, ("S", i, a))
                dve.sem_inc(Q["S"], 1)
            dve.wait_ge(Q["sq"], 4 * i + 4)
            TS(VAR2, SS2, 1.0 / P, EPS, ALU.mult, ALU.add).then_inc(Q["var"], 1)
            dve.wait_ge(Q["sd"], i + 1)
            link(dve.reciprocal(RS2, SD2))
            TT(on[:, :, :], heads(bank(("O", i))), over(RS2), ALU.mult).then_inc(seen(("O", i)), 1)
            read_done(dve, ("O", i))
            dve.sem_inc(Q["on"], 1)
            filled(dve, ("oT", i))
            STT(out=proj2[:, 8:12, c], in0=heads(bank(("oT", i))), scalar=vc("gdn_gain"), in1=proj2[:, 13:17, c],
                op0=ALU.mult, op1=ALU.mult).then_inc(seen(("oT", i)), 1)
            read_done(dve, ("oT", i))
            dve.sem_inc(gdn_done, 1)

        def nsa_dve_(dve, link):
            TT, TS, STT = dve.tensor_tensor, dve.tensor_scalar, dve.scalar_tensor_tensor
            dve.wait_ge(const3_in, 160)
            for k, s_ in enumerate(ROPED):
                tag = ("rope", k)
                filled(dve, tag)
                TT(rtmp[:, k % 2, :], bank(tag), sinT[:, :], ALU.mult).then_inc(seen(tag), 1)
                link(TT(proj2[:, s_, :], proj2[:, s_, :], cosT[:, :], ALU.mult))
                link(TT(proj2[:, s_, :], proj2[:, s_, :], rtmp[:, k % 2, :], ALU.add))
            for dst, s_ in ((kds, 23), (kdw, 25)):
                for g in range(2):
                    for r in range(2):
                        TS(dst[64 * r:64 * r + 64, g, :], proj2[64 * g:64 * g + 64, s_, :], 0.125, None, ALU.mult)\
                            .then_inc(Q2["keys"], 1)
            for b, s_ in enumerate((21, 22)):
                for g in range(2):
                    for par in range(2):
                        for m in range(2):
                            src = proj2[64 * g:64 * g + 64, s_, :].rearrange("p (n r two) -> p two r n", r=8, two=2)
                            pos = posT[64 * par:64 * par + 64, b, 8 * m:8 * m + 8].unsqueeze(2).to_broadcast([64, 8, 31])
                            dst = blk[b][64 * par:64 * par + 64, 8 * m:8 * m + 8, 31 * g:31 * g + 31]
                            if par == g:
                                TT(dst, src[:, par, :, m:m + 31], pos, ALU.add).then_inc(Q2["blk"], 1)
                            else:
                                link(TS(dst, src[:, par, :, m:m + 31], 1.0, None, ALU.mult))
                                TT(dst, dst, pos, ALU.add).then_inc(Q2["blk"], 1)

            def front(n):
                i, g, hp, br = STEPS[n]
                W = keys_of(br, i)
                b0 = USES[("sc", n)][1]
                b = n % 2
                filled(dve, ("sc2", n))
                both = psx[:, b0:b0 + 2, :]
                if br == 0:
                    link(TT(both[:, :, 0:31], both[:, :, 0:31], cmask[:, i:i + 1, :].to_broadcast([P, 2, 31]), ALU.add))
                else:
                    link(TT(both[:, :, icols(i)], both[:, :, icols(i)],
                            dmask[:, :].unsqueeze(1).to_broadcast([P, 2, P]), ALU.add))
                dve.tensor_reduce(stat[:, 220 + 2 * b:222 + 2 * b], both[:, :, 0:W], AX_X, ALU.max, negate=True)\
                   .then_inc(sm_max, 1)

            def back(n):
                i, g, hp, br = STEPS[n]
                W = keys_of(br, i)
                b = n % 2
                read_done(dve, ("sc", n))
                read_done(dve, ("sc2", n))
                link(dve.reciprocal(stat[:, 228 + 2 * b:230 + 2 * b], stat[:, 224 + 2 * b:226 + 2 * b]))
                g0 = 64 + 12 * g + 6 * hp + br
                for par in range(2):
                    ins = TS(scale[b][:, par, :], ident[:, :], smalltok[:, i, g0 + 3 * par:g0 + 3 * par + 1],
                             stat[:, 228 + 2 * b + par:229 + 2 * b + par], ALU.mult, ALU.mult)
                ins.then_inc(scale_made, 1)

            for g in range(2):
                link(TS(smalltok[:, 0, 64 + 12 * g:76 + 12 * g:3], smalltok[:, 0, 64 + 12 * g:76 + 12 * g:3],
                        rowvis[:, :], None, ALU.mult))
            front(0)
            front(1)
            for n, (i, g, hp, br) in enumerate(STEPS):
                back(n)
                if n + 2 < len(STEPS):
                    front(n + 2)
                if hp == 1 and br == 2:
                    tag = ("o", i, g)
                    filled(dve, tag)
                    ps = bank(tag)[0:64, :].rearrange("p (a b c) -> p a b c", b=2, c=P)
                    for r in range(2):
                        ins = dve.tensor_copy(proj2[64 * r:64 * r + 64, 17 + 2 * g:19 + 2 * g, icols(i)], ps[:, :, r, :])
                    ins.then_inc(seen(tag), 1)
            read_done(dve, ("o", NT - 1, 1))
            dve.sem_inc(nsa_done, 1)

        block = ctx.enter_context(nc.Block())

        @block.sync
        def _(sp):
            sp.dma_start(hres[:, :, :], t["x"].rearrange("(i p) d -> p i d", p=P)).then_inc(x_in, 16)
            for dst, src in ((vec, t["vec"]), (ident, t["ident"]), (relneg, t["relneg"]), (tri, t["tri"]),
                             (desc, t["desc"])):
                sp.dma_start(dst[:, :], src).then_inc(const_in, 16)
            sp.dma_start(wr[:, :, :], t["w_router"].rearrange("(k p) c -> p k c", p=P)).then_inc(const_in, 16)
            sp.dma_start(rbias[:, :], t["b_router"].partition_broadcast(P)).then_inc(const_in, 16)
            sp.dma_start(sinkb[:, :], t["sinks"].partition_broadcast(P)).then_inc(const_in, 16)
            load_slabs(sp, "in1", 2)
            sp.wait_ge(zero_set, 2)
            zeros = zero[0:BLK, :].unsqueeze(1).to_broadcast([BLK, 8, 128])
            sp.dma_start(xs_dram[ASSIGN:XS_ROWS, :].rearrange("p (a c) -> p a c", c=128), zeros).then_inc(tail_stored, 16)
            for m in range(XS_ROWS // BLK):
                r0 = YS_OVER + BLK * m
                sp.dma_start(ys_dram[r0:r0 + BLK, :].rearrange("p (a c) -> p a c", c=128), zeros).then_inc(tail_stored, 16)
            load_slabs(sp, "gates1")
            load_slabs(sp, "attn_out")
            load_slabs(sp, "conv_out")
            load_slabs(sp, "out1")
            load_slabs(sp, "small2")
            sp.wait_ge(res_added, 16)
            sp.dma_start(gb[:, :], t["g_ffn_row"].partition_broadcast(P)).then_inc(gb_in, 16)

            def expert_weights(e, b, half):
                for h in range(2):
                    sp.dma_start(wgu[b][:, 4 * h:4 * h + 4, 0:FF],
                                 t["w_gate"][bass.ds(e, 1), 512 * h:512 * h + 512, :]
                                 .rearrange("e (k p) f -> p (e k) f", p=P)).then_inc(gu_in[b], 16)
                    sp.dma_start(wgu[b][:, 4 * h:4 * h + 4, FF:2 * FF],
                                 t["w_up"][bass.ds(e, 1), 512 * h:512 * h + 512, :]
                                 .rearrange("e (k p) f -> p (e k) f", p=P)).then_inc(gu_in[b], 16)

            def expert_down(e, b):
                sp.dma_start(wd[b][:, :, :], t["w_down"][bass.ds(e, 1), :, :]
                             .rearrange("e (k p) f -> p (e k) f", p=P)).then_inc(wd_in[b], 16)

            def expert_rows(e, b):
                row = sp.value_load(idx[0:1, bass.ds(16 + e, 1)], min_val=0, max_val=ASSIGN)
                for h in range(2):
                    sp.dma_start(xg[b][64 * h:64 * h + 64, :], xs_dram[bass.ds(row, BLK), 512 * h:512 * h + 512])\
                      .then_inc(xg_in[b], 16)

            expert_weights(0, 0, 0)
            expert_down(0, 0)
            sp.wait_ge(logits_made, 1)
            expert_weights(1, 1, 0)
            sp.wait_ge(dest_made, 1)
            sp.wait_ge(tail_stored, 16 * (1 + XS_ROWS // BLK))
            sp.wait_ge(rows_scattered, 16 * 2 * NT)
            expert_rows(0, 0)
            expert_down(1, 1)
            expert_rows(1, 1)
            with sp.Fori(1, NE // 2) as i:
                for b in range(2):
                    e = 2 * i + b
                    sp.wait_ge(gu_full, e - 1)
                    expert_weights(e, b, i)
                    sp.wait_ge(xgT_full, e - 1)
                    sp.wait_ge(dest_made, 1)
                    expert_rows(e, b)
                    sp.wait_ge(y_full, e - 1)
                    expert_down(e, b)
            sp.wait_ge(y_full, NE)
            for b in range(2):
                sp.wait_ge(y_stored[b], 16 * NE)
            more = sp.value_load(idx[0:1, 48:49], min_val=0, max_val=OVER)
            with sp.If(more > 0):
                sp.sem_inc(o_stored, 1)
                with sp.Fori(0, OVER) as j:
                    e = sp.value_load(ovi[0:1, bass.ds(j, 1)], min_val=0, max_val=NE - 1)
                    row = sp.value_load(ovi[0:1, bass.ds(16 + j, 1)], min_val=0, max_val=ASSIGN)
                    sp.wait_ge(o_stored, 32 * j + 1)
                    for w, c in (("w_gate", 0), ("w_up", FF)):
                        sp.dma_start(wgu[0][:, :, c:c + FF], t[w][bass.ds(e, 1), :, :]
                                     .rearrange("e (k p) f -> p (e k) f", p=P)).then_inc(o_in, 16)
                    sp.dma_start(wd[0][:, :, :], t["w_down"][bass.ds(e, 1), :, :]
                                 .rearrange("e (k p) f -> p (e k) f", p=P)).then_inc(o_in, 16)
                    for h in range(2):
                        sp.dma_start(xg[0][64 * h:64 * h + 64, :], xs_dram[bass.ds(row, BLK), 512 * h:512 * h + 512])\
                          .then_inc(o_in, 16)
                    sp.wait_ge(yo_made, NE + j + 1)
                    for h in range(2):
                        sp.dma_start(ys_dram[bass.ds(YS_OVER + row, BLK), 512 * h:512 * h + 512],
                                     yo[0][64 * h:64 * h + 64, :]).then_inc(o_stored, 16)
                sp.wait_ge(o_stored, 32 * OVER + 1)
            sp.sem_inc(over_done, 1)
            sp.dma_start(gfb[:, :], t["g_final_row"].partition_broadcast(P)).then_inc(gf_in, 16)
            load_slabs(sp, "in2q")
            sp.wait_ge(final1_made, NT)
            for dst, src in ((gmask[:, :, :], t["gmask"]), (sel[:, :, :], t["sel"])):
                sp.dma_start(dst, src).then_inc(const2_in, 16)
            sp.dma_start(cgo[:, :], t["chunk_go"].partition_broadcast(P)).then_inc(const2_in, 16)
            load_slabs(sp, "in2n")
            load_slabs(sp, "in2m", 1, "peeled")
            sp.wait_ge(gdn_done, NT)
            for dst, src in ((cosT, "cos"), (sinT, "sin"), (rotp, "rot"), (dmask, "dmask"), (cmask, "cmask"),
                             (rowvis, "rowvis"), (posT, "pos"), (w2s, "w2")):
                sp.dma_start(dst[tuple([slice(None)] * len(dst.shape))], t[src])\
                  .then_inc(const3_in, 16)
            for b, n in enumerate(("cmp_w1_k_2", "cmp_w1_v_2")):
                sp.dma_start(w1[b][:, :, :], t[n].rearrange("(a p) h -> p a h", p=P)).then_inc(const3_in, 16)
            load_slabs(sp, "in2m", 1, "rest")
            for name in ("gdn_out", "nsa_out", "out2", "gate_up", "down"):
                load_slabs(sp, name)
            sp.wait_ge(down_used, 11)
            sp.dma_start(goutb[:, :], t["final_gain_row"].partition_broadcast(P)).then_inc(gout_in, 16)
            for i in range(NT):
                sp.wait_ge(out_made, i + 1)
                sp.dma_start(t["out"][i * P:(i + 1) * P, :], fin[:, i, :]).then_inc(out_stored, 16)
            sp.wait_ge(out_stored, 16 * NT)

        @block.gpsimd
        def _(pool):
            pool.memset(vpad[:, :, :], 0.0).then_inc(ones_set, 1)
            pool.memset(ones[:, :], 1.0 / 512).then_inc(ones_set, 1)
            pool.memset(one[:, :], 1.0).then_inc(ones_set, 1)
            pool.memset(zero[:, :], 0.0).then_inc(zero_set, 1)
            pool.memset(stat[:, 140:141], EPS).then_inc(zero_set, 1)
            split_lo(pool, "in1", 2)
            split_lo(pool, "gates1")
            split_lo(pool, "attn_out")
            split_lo(pool, "conv_out")
            split_lo(pool, "out1")
            split_lo(pool, "small2")
            pool.wait_ge(xt_made, NT)
            pool.wait_ge(dest_made, 1)
            for i in range(NT):
                for k in range(2):
                    pool.indirect_dma_start(out=xs_dram, out_offset=bass.IndirectOffsetOnAxis(ap=idx[:, 2 * i + k:2 * i + k + 1], axis=0),
                                            in_=xt[:, i, :], in_offset=None).then_inc(rows_scattered, 16)
            pool.wait_ge(over_done, 1)
            for c in range(2 * NT):
                pool.indirect_dma_start(out=yg[c][:, :], out_offset=None, in_=ys_dram,
                                        in_offset=bass.IndirectOffsetOnAxis(ap=idx[:, 8 + c:9 + c], axis=0))\
                    .then_inc(rows_gathered[c], 16)
            split_lo(pool, "in2q")
            split_lo(pool, "in2n", 3, "peeled")
            for i in range(NT):
                for l in range(1, LEVELS):
                    if l == 1:
                        pool.wait_ge(gdn_at, i + 1)
                    if l > 2:
                        filled(pool, ("P1", i, l - 2))
                    pool.tensor_tensor(AL[l % 2][:, :, :], AT[:, :, :], gm(2 + l), ALU.mult).then_inc(gdn_pool, 1)
                if i < 2:
                    split_slab_lo(pool, "in2n", 3 + i, slab_place("in2n", 3 + i)[1])
            for name in ("in2m", "gdn_out", "nsa_out", "out2", "gate_up", "down"):
                split_lo(pool, name)

        @block.scalar
        def _(act):
            steps = [0]

            def link(ins):
                steps[0] += 1
                ins.then_inc(act_step, 1)
                act.wait_ge(act_step, steps[0])

            norm_act(act, 0, hres, lambda e: e.wait_ge(x_in, 16), xn)
            act.wait_ge(const_in, 128)
            for k in range(KD):
                act.wait_ge(tile_full, RING["xn1"] + k + 1)
                act.activation(acthi[:, k, :], psg[:, k % 2, :], ACT.Copy, scale=vc("g_mix", k)).then_inc(hi_made, 1)
            split_hi(act, 2048, 0, 0, 0)

            def copy_tiles(j, half, par):
                for f in range(2):
                    T = RING["in1"] + f
                    act.wait_ge(tile_full, T + 2 * j + 1)
                    act.activation(proj[:, 2 * j + f, :], psg[:, T % 2, :], ACT.Sigmoid if 2 <= j < 4 else ACT.Copy)\
                       .then_inc(tile_free[T % 2], 1)
            each_slab_act(act, "in1", copy_tiles, 7)

            def unit_exps(u):
                W = 128 if u < 2 else 256
                act.wait_ge(negmax_made, u + 1)
                for h in range(4):
                    act.activation(sc[u % 2][:, h, 0:W], sc[u % 2][:, h, 0:W], ACT.Exp,
                                   bias=stat[:, 64 + 4 * (u % 2) + h:65 + 4 * (u % 2) + h],
                                   accum_out=stat[:, 80 + 4 * (u % 2) + h:81 + 4 * (u % 2) + h]).then_inc(exps_made, 1)
                act.activation(stat[:, 104 + 4 * (u % 2):108 + 4 * (u % 2)],
                               stat[:, 96 + 4 * (u % 2):100 + 4 * (u % 2)], ACT.Exp).then_inc(exps_made, 1)

            def unit_probsT(u):
                W = 128 if u < 2 else 256
                act.wait_ge(probsT_full, u + 1)
                if u >= 2:
                    act.wait_ge(heads_full, u - 1)
                act.activation(pT[u % 2][:, 0:W // P, :], psx[:, 2:2 + W // P, :], ACT.Copy).then_inc(probsT_copied, 1)

            def gates_and_unit(j, half, par):
                for f in range(2):
                    T = RING["gates1"] + 2 * j + f
                    act.wait_ge(tile_full, T + 1)
                    act.activation(proj[:, 14 + 2 * j + f, :], psg[:, T % 2, :], ACT.Copy).then_inc(tile_free[T % 2], 1)
                    if j == 0 and f == 0:
                        act.wait_ge(vtok_full, 1)
                        act.activation(vtok[:, :, :], psx[:, 5, :].rearrange("p (i c) -> p i c", c=P), ACT.Copy)\
                           .then_inc(vtok_made, 1)
                if j >= 1:
                    unit_probsT(j - 1)
                unit_exps(j)
            each_slab_act(act, "gates1", gates_and_unit, 8)
            unit_probsT(7)
            for b in range(2):
                act.wait_ge(tile_free[b], freed(b, RING["attn_out"]))
            act.activation(proj[:, 22:30, :], proj[:, 22:30, :], ACT.Sigmoid).then_inc(gates_sig, 1)
            act.wait_ge(heads_copied, 16)
            act.activation(acthi[:, 4:8, :], attnT[:, :, :], ACT.Copy).then_inc(attn_hi, 1)
            for k in range(4):
                act.wait_ge(conv_centred, k + 1)
                act.activation(proj[:, k, :], proj[:, 4 + k, :], ACT.Square).then_inc(conv_sq, 1)
            act.activation(proj[:, 14:22, :], proj[:, 14:22, :], ACT.Sigmoid).then_inc(gates_sig, 1)
            next_hi(act, "attn_out", 0, *slab_place("attn_out", 0))
            act.wait_ge(conv_var, 1)
            act.activation(vpad[:, 1, 0:SEQ], vpad[:, 0, 0:SEQ], ACT.Sqrt).then_inc(conv_sd, 1)
            act.wait_ge(conv_norm, 4)
            for k in range(4):
                act.activation(proj[:, k, :], proj[:, 4 + k, :], ACT.Silu, bias=vc("ln_b", k),
                               scale=vc("ln_g", k)).then_inc(conv_act, 1)
            act.wait_ge(conv_act, 4)
            act.activation(acthi[:, 0:4, :], proj[:, 0:4, :], ACT.Copy).then_inc(conv_split, 1)
            next_hi(act, "attn_out", 1, *slab_place("attn_out", 1))

            def merged_upper(j, half, par):
                for f in range(4):
                    act.wait_ge(merged_made, 4 * j + f + 1)
                    act.activation(act2hi[:, 4 * j + f, :], proj[:, 14 + 4 * j + f, :], ACT.Copy).then_inc(merged_hi, 1)
            each_slab_act(act, "conv_out", merged_upper)
            each_slab_act(act, "out1", lambda j, half, par: None)
            norm_act(act, 1, hres, lambda e: e.wait_ge(res_added, 16), xt)
            for k in range(0, KD, 2):
                T = RING["xnffn"] + k
                act.wait_ge(tile_full, T + 1)
                act.activation(xtT[:, k, :], psg[:, T % 2, :], ACT.Copy).then_inc(tile_free[T % 2], 1)
            T = RING["router"]
            act.wait_ge(tile_full, T + 1)
            act.activation(rt[0:36, 0:4, :], psg[0:36, T % 2, :].rearrange("p (a b) -> p a b", b=P), ACT.Copy)\
               .then_inc(tile_free[T % 2], 1)
            act.wait_ge(route_dve, 1)
            act.activation(rt[:, 13, 16:32], rt[:, 13, 0:16], ACT.Exp).then_inc(route_act, 1)
            act.wait_ge(route_dve, 2)
            act.activation(rt[:, 13, 52:56], rt[:, 13, 48:52], ACT.Exp).then_inc(route_act, 1)

            def expert_act(e, b, stored, sems, full_gu, full_y, store=True):
                s_gu, s_sg, s_hmT_full, s_hmT, s_y, s_yo = sems
                act.wait_ge(s_gu, e + 1)
                act.activation(sg[64:128, :], psx[0:64, full_gu, :], ACT.Silu).then_inc(s_sg, 1)
                act.wait_ge(s_hmT_full, e + 1)
                act.activation(hmT[b][:, :, :], psx[:, 3, :].rearrange("p (a b) -> p a b", b=P)[:, :, BLK:P], ACT.Copy)\
                   .then_inc(s_hmT, 1)
                act.wait_ge(s_y, e + 1)
                if stored is not None:
                    act.wait_ge(y_stored[b], stored)
                act.activation(yo[b][:, :], psx[:, full_y, :], ACT.Copy).then_inc(s_yo, 1)
                if store:
                    act.wait_ge(yo_made, e + 1)
                    for h in range(2):
                        act.dma_start(ys_dram[bass.ds(BLK * e, BLK), 512 * h:512 * h + 512],
                                      yo[b][64 * h:64 * h + 64, :]).then_inc(y_stored[b], 16)

            main = (gu_full, sg_made, hmT_full, hmT_made, y_full, yo_made)
            for e in range(2):
                expert_act(e, e, None, main, e, 4 + e)
            with act.Fori(1, NE // 2) as i:
                for b in range(2):
                    expert_act(2 * i + b, b, 32 * i, main, b, 4 + b)
            more = act.value_load(idx[0:1, 48:49], min_val=0, max_val=OVER)
            with act.If(more > 0):
                with act.Fori(0, OVER) as j:
                    expert_act(NE + j, 0, None, main, 0, 4, store=False)
            block2_act(act, link)

        @block.tensor
        def _(pe):
            pe.wait_ge(const_in, 128)
            transposes_of(pe, "xn1", xn, xn_made, NT)
            pe.wait_ge(lo_made, 8)
            features_by_tokens(pe, "in1", acthi, actlo, 2)

            def scores(u):
                n, g = u // 2, u % 2
                lo = (n - 1) * P if n else 0
                if u == 0:
                    pe.wait_ge(kdup_made, 4)
                else:
                    pe.wait_ge(scores_read, u)
                for h in range(4):
                    head = 4 * g + h
                    r = 64 * (head % 2)
                    W = (n + 1) * P - lo
                    mm = pe.matmul(psx[:, 0:2, :].rearrange("p a (b c) -> p (a b) c", c=256)[:, slot(h), 0:W],
                                   proj[r:r + 64, 8 + head // 2, n * P:(n + 1) * P],
                                   kdup[r:r + 64, g, lo:(n + 1) * P], start=True, stop=True)
                mm.then_inc(scores_full, 1)

            def probs_T(u):
                pe.wait_ge(probs_made, u + 1)
                if u >= 1:
                    pe.wait_ge(probsT_copied, u)
                for a in range(1 if u < 2 else 2):
                    for h in range(4):
                        mm = pe.transpose(psx[:, 2 + a, h * P:(h + 1) * P], sc[u % 2][:, h, a * P:(a + 1) * P], ident[:, :])
                mm.then_inc(probsT_full, 1)

            def values(u):
                n, g = u // 2, u % 2
                halves = 1 if n == 0 else 2
                pe.wait_ge(probsT_copied, u + 1)
                if u >= 1:
                    pe.wait_ge(heads_copied, 2 * u)
                else:
                    pe.wait_ge(vtok_made, 1)
                for a in range(halves):
                    mm = pe.matmul(psx[0:64, 4, :], vtok[:, n - halves + 1 + a, g * 64:(g + 1) * 64], pT[u % 2][:, a, :],
                                   start=(a == 0), stop=(a == halves - 1))
                mm.then_inc(heads_full, 1)

            def attention_steps(j, f):
                if f == 0:
                    if j == 0:
                        for b in range(2):
                            pe.wait_ge(tile_free[b], freed(b, RING["gates1"]))
                        for i in range(NT):
                            mm = pe.transpose(psx[:, 5, i * P:(i + 1) * P], proj[:, 13, i * P:(i + 1) * P], ident[:, :])
                        mm.then_inc(vtok_full, 1)
                    if j >= 2:
                        values(j - 2)
                    scores(j)
                elif j >= 1:
                    probs_T(j - 1)
            features_by_tokens(pe, "gates1", acthi, actlo, after=attention_steps)
            values(6)
            probs_T(7)
            values(7)
            pe.wait_ge(conv_tap, 124)
            pe.wait_ge(ones_set, 2)
            for k in range(4):
                mm = pe.matmul(psx[:, 5, :], ones[:, :], proj[:, 4 + k, :], start=(k == 0), stop=(k == 3))
            mm.then_inc(mean_full, 1)

            def square_means(j, f):
                if j == 0 and f == 3:
                    pe.wait_ge(scores_read, 8)
                    for k in range(4):
                        pe.wait_ge(conv_sq, k + 1)
                        mm = pe.matmul(psx[:, 0, :], ones[:, :], proj[:, k, :], start=(k == 0), stop=(k == 3))
                    mm.then_inc(square_mean_full, 1)
            pe.wait_ge(attn_split, 1)
            features_by_tokens(pe, "attn_out", acthi[:, 4:8, :], actlo[:, 4:8, :], after=square_means)
            pe.wait_ge(conv_split, 2)
            features_by_tokens(pe, "conv_out", acthi, actlo)
            pe.wait_ge(merged_lo, 8)
            tokens_by_features(pe, "out1", act2hi, act2lo)
            transposes_of(pe, "xnffn", xt, xt_made, NT)
            T = RING["router"]
            for b in range(2):
                pe.wait_ge(tile_free[b], freed(b, T))
            for k in range(KD):
                mm = pe.matmul(psg[0:36, T % 2, :], wr[:, k, :], xtT[:, k, :], start=(k == 0), stop=(k == KD - 1))
            mm.then_inc(tile_full, 1)
            T = RING["router_t"]
            pe.wait_ge(tile_free[1 - T % 2], freed(1 - T % 2, T))
            for i in range(NT):
                mm = pe.transpose(psg[:, T % 2, 36 * i:36 * i + 36], rt[0:36, i, :], ident[0:36, 0:36])
            mm.then_inc(tile_full, 1)
            T = RING["rank"]
            pe.wait_ge(picks_made, 1)
            pe.wait_ge(tile_free[T % 2], T // 2)
            pe.matmul(psg[:, T % 2, 0:128], tri[:, :], rt[:, 11, :], start=True, stop=True)
            pe.matmul(psg[:, T % 2, 128:256], one[:, :], rt[:, 11, :], start=True, stop=True).then_inc(tile_full, 1)

            def rows_T(e, b, s_in, n_in, s_made, s_full):
                pe.wait_ge(s_in, n_in)
                if not isinstance(e, int) or e > 0:
                    pe.wait_ge(s_made, e)
                for k in range(4):
                    mm = pe.transpose(psx[:, 2, P * k:P * k + P], xg[b][:, k * P:(k + 1) * P], ident[:, :])
                mm.then_inc(s_full, 1)

            def gate_up(e, b, s_made, s_full, s_in, n_in):
                pe.wait_ge(s_in, n_in)
                pe.wait_ge(s_made, e + 1)
                for k in range(KD):
                    for h in range(2):
                        mm = pe.matmul(psx[64 * h:64 * h + 64, b, :], xgT[b][:, k, :], wgu[b][:, k, FF * h:FF * h + FF],
                                       start=(k == 0), stop=(k == KD - 1))
                mm.then_inc(s_full, 1)

            def hidden_T(e, b, s_hm, s_full, s_made):
                pe.wait_ge(s_hm, e + 1)
                for k in range(FF // P):
                    mm = pe.transpose(psx[:, 3, P * k:P * k + P], hm[:, k * P:(k + 1) * P], ident[:, :])
                mm.then_inc(s_full, 1)

            def down(e, b, s_made, s_full):
                pe.wait_ge(s_made, e + 1)
                for k in range(FF // P):
                    for h in range(2):
                        mm = pe.matmul(psx[64 * h:64 * h + 64, 4 + b, :], hmT[b][:, k, :],
                                       wd[b][:, k, 512 * h:512 * h + 512], start=(k == 0), stop=(k == FF // P - 1))
                mm.then_inc(s_full, 1)

            def expert_pe(e, b, half, last=False, first=False):
                if not first:
                    pe.wait_ge(hm_made, e - 1)
                gate_up(e, b, xgT_made, gu_full, gu_in[b], 64 * half + 64)
                if not last:
                    rows_T(e + 1, 1 - b, xg_in[1 - b], 32 * (half + b) + 32, xgT_made, xgT_full)
                hidden_T(e, b, hm_made, hmT_full, hmT_made)
                pe.wait_ge(wd_in[b], 16 * half + 16)
                if not first:
                    pe.wait_ge(yo_made, e - 1)
                down(e, b, hmT_made, y_full)

            pe.wait_ge(hm_cleared, 1)
            rows_T(0, 0, xg_in[0], 32, xgT_made, xgT_full)
            expert_pe(0, 0, 0, first=True)
            expert_pe(1, 1, 0, first=True)
            with pe.Fori(1, NE // 2 - 1) as i:
                for b in range(2):
                    expert_pe(2 * i + b, b, i)
            expert_pe(NE - 2, 0, NE // 2 - 1)
            expert_pe(NE - 1, 1, NE // 2 - 1, last=True)
            more = pe.value_load(idx[0:1, 48:49], min_val=0, max_val=OVER)
            with pe.If(more > 0):
                pe.wait_ge(yo_made, NE)
                with pe.Fori(0, OVER) as j:
                    pe.wait_ge(o_in, 80 * j + 80)
                    for k in range(4):
                        mm = pe.transpose(psx[:, 2, P * k:P * k + P], xg[0][:, k * P:(k + 1) * P], ident[:, :])
                    mm.then_inc(xgT_full, 1)
                    gate_up(NE + j, 0, xgT_made, gu_full, o_in, 80 * j + 80)
                    hidden_T(NE + j, 0, hm_made, hmT_full, hmT_made)
                    down(NE + j, 0, hmT_made, y_full)
            block2_pe(pe)

        @block.vector
        def _(dve):
            steps = [0]

            def link(ins):
                steps[0] += 1
                ins.then_inc(dve_step, 1)
                dve.wait_ge(dve_step, steps[0])

            norm_dve(dve, 0)
            dve.wait_ge(norm_rs, 1)
            for i in range(NT):
                dve.tensor_scalar(xn[:, i, :], hres[:, i, :], rstd(0, i), None, ALU.mult).then_inc(xn_made, 1)
            for k in range(KD):
                dve.wait_ge(hi_made, k + 1)
                dve.scalar_tensor_tensor(out=actlo[:, k, :], in0=psg[:, k % 2, :], scalar=vc("g_mix", k),
                                         in1=acthi[:, k, :].bitcast(F32), op0=ALU.mult, op1=ALU.subtract)\
                   .then_inc(tile_free[k % 2], 1)
            dve.wait_ge(tile_free[0], 4)
            dve.wait_ge(tile_free[1], 4)
            dve.sem_inc(lo_made, 8)
            for b in range(2):
                dve.wait_ge(tile_free[b], freed(b, RING["in1"] + 8))
            for k in range(4):
                dve.tensor_tensor(vpad[:, k, 30:30 + SEQ], proj[:, k, :], proj[:, 4 + k, :], ALU.mult).then_inc(conv_v, 1)
            dve.wait_ge(ones_set, 1)
            dve.wait_ge(conv_v, 4)
            for k in range(4):
                dve.tensor_scalar(proj[:, 4 + k, :], vpad[:, k, 0:SEQ], vc("w_dw", 31 * k), vc("b_dw", k), ALU.mult,
                                  ALU.add).then_inc(conv_tap, 1)

            def tap(j):
                for k in range(4):
                    dve.wait_ge(conv_tap, 4 * j - 3 + k)
                    dve.scalar_tensor_tensor(out=proj[:, 4 + k, :], in0=vpad[:, k, bass.ds(j, SEQ)],
                                             scalar=vec[:, bass.ds(VEC["w_dw"][0] + 31 * k + j, 1)],
                                             in1=proj[:, 4 + k, :], op0=ALU.mult, op1=ALU.add).then_inc(conv_tap, 1)
            BEFORE = 13
            with dve.Fori(1, BEFORE) as j:
                tap(j)
            for b in range(2):
                dve.wait_ge(tile_free[b], freed(b, RING["gates1"]))
            for g in range(2):
                for r in range(2):
                    dve.tensor_scalar(kdup[64 * r:64 * r + 64, g, :], proj[64 * g:64 * g + 64, 12, :], 0.125, None,
                                      ALU.mult).then_inc(kdup_made, 1)
            def soft_front(u):
                n, g = u // 2, u % 2
                W = 128 if n == 0 else 256
                b = u % 2
                if u >= 2:
                    dve.wait_ge(probsT_full, u - 1)
                dve.wait_ge(scores_full, u + 1)
                sc_ps = psx[:, 0:2, :].rearrange("p a (b c) -> p (a b) c", c=256)
                for h in range(4):
                    ins = dve.scalar_tensor_tensor(out=sc[b][:, h, 0:W], in0=relneg[:, 256 - W:256],
                                                   scalar=SLOPES[4 * g + h], in1=sc_ps[:, slot(h), 0:W],
                                                   op0=ALU.mult, op1=ALU.add)
                ins.then_inc(scores_read, 1)
                dve.wait_ge(scores_read, u + 1)
                link(dve.tensor_reduce(stat[:, 112:116], sc[b][:, :, 0:W], AX_X, ALU.max))
                link(dve.tensor_tensor(stat[:, 116:120], stat[:, 112:116], sinkb[:, 4 * g:4 * g + 4], ALU.max))
                link(dve.tensor_scalar(stat[:, 64 + 4 * b:68 + 4 * b], stat[:, 116:120], -1.0, None, ALU.mult))
                dve.tensor_tensor(stat[:, 96 + 4 * b:100 + 4 * b], sinkb[:, 4 * g:4 * g + 4],
                                  stat[:, 64 + 4 * b:68 + 4 * b], ALU.add).then_inc(negmax_made, 1)

            def soft_back(u):
                n, g = u // 2, u % 2
                W = 128 if n == 0 else 256
                b = u % 2
                dve.wait_ge(exps_made, 5 * (u + 1))
                link(dve.tensor_tensor(stat[:, 120:124], stat[:, 80 + 4 * b:84 + 4 * b],
                                       stat[:, 104 + 4 * b:108 + 4 * b], ALU.add))
                link(dve.reciprocal(stat[:, 124:128], stat[:, 120:124]))
                dve.tensor_tensor(sc[b][:, :, 0:W], sc[b][:, :, 0:W],
                                  stat[:, 124:128].unsqueeze(2).to_broadcast([P, 4, W]), ALU.mult).then_inc(probs_made, 1)

            def heads_out(u):
                n, g = u // 2, u % 2
                dve.wait_ge(heads_full, u + 1)
                ps = psx[0:64, 4, :].rearrange("p (a b c) -> p a b c", b=2, c=P)
                for r in range(2):
                    dve.tensor_copy(attnT[64 * r:64 * r + 64, 2 * g:2 * g + 2, n * P:(n + 1) * P],
                                    ps[:, :, r, :]).then_inc(heads_copied, 1)

            soft_front(0)
            for u in range(8):
                taps = [BEFORE + (31 - BEFORE) * v // 16 for v in (2 * u, 2 * u + 1, 2 * u + 2)]
                for j in range(taps[0], taps[1]):
                    tap(j)
                soft_back(u)
                for j in range(taps[1], taps[2]):
                    tap(j)
                if u < 7:
                    soft_front(u + 1)
                if u >= 1:
                    heads_out(u - 1)
            heads_out(7)
            dve.wait_ge(attn_hi, 1)
            dve.tensor_tensor(actlo[:, 4:8, :], attnT[:, :, :], acthi[:, 4:8, :].bitcast(F32), ALU.subtract)\
               .then_inc(attn_split, 1)

            def gated_attention(fs):
                for f in fs:
                    T = RING["attn_out"] + f
                    dve.wait_ge(tile_full, T + 1)
                    dve.tensor_tensor(proj[:, 22 + f, :], psg[:, T % 2, :], proj[:, 22 + f, :], ALU.mult)\
                       .then_inc(tile_free[T % 2], 1)
            dve.wait_ge(mean_full, 1)
            for k in range(4):
                dve.tensor_tensor(proj[:, 4 + k, :], proj[:, 4 + k, :], psx[:, 5, :], ALU.subtract)\
                   .then_inc(conv_centred, 1)
            dve.wait_ge(gates_sig, 1)
            gated_attention(range(0, 4))
            dve.wait_ge(square_mean_full, 1)
            dve.tensor_scalar(vpad[:, 0, 0:SEQ], psx[:, 0, :], EPS, None, ALU.add).then_inc(conv_var, 1)
            dve.wait_ge(conv_sd, 1)
            link(dve.reciprocal(vpad[:, 2, 0:SEQ], vpad[:, 1, 0:SEQ]))
            for k in range(4):
                dve.tensor_tensor(proj[:, 4 + k, :], proj[:, 4 + k, :], vpad[:, 2, 0:SEQ], ALU.mult).then_inc(conv_norm, 1)
            dve.wait_ge(conv_split, 1)
            dve.tensor_tensor(actlo[:, 0:4, :], proj[:, 0:4, :], acthi[:, 0:4, :].bitcast(F32), ALU.subtract)\
               .then_inc(conv_split, 1)
            gated_attention(range(4, 8))
            for b in range(2):
                dve.wait_ge(tile_free[b], freed(b, RING["attn_out"] + 8))
            dve.wait_ge(gates_sig, 2)
            for f in range(8):
                T = RING["conv_out"] + f
                dve.wait_ge(tile_full, T + 1)
                dve.tensor_tensor(proj[:, 14 + f, :], psg[:, T % 2, :], proj[:, 14 + f, :], ALU.mult)\
                   .then_inc(tile_free[T % 2], 1)
                dve.wait_ge(tile_free[T % 2], T // 2 + 1)
                dve.tensor_tensor(proj[:, 14 + f, :], proj[:, 14 + f, :], proj[:, 22 + f, :], ALU.add)\
                   .then_inc(merged_made, 1)
                dve.wait_ge(merged_hi, f + 1)
                dve.tensor_tensor(act2lo[:, f, :], proj[:, 14 + f, :], act2hi[:, f, :].bitcast(F32), ALU.subtract)\
                   .then_inc(merged_lo, 1)

            def add_residual(j, half, par):
                for i in range(NT):
                    T = RING["out1"] + i
                    dve.wait_ge(tile_full, T + 4 * j + 1)
                    dst = hres[:, i, bass.ds(256 * j, 256)]
                    dve.tensor_tensor(dst, dst, psg[:, T % 2, 0:256], ALU.add).then_inc(tile_free[T % 2], 1)
            each_slab(dve, "out1", add_residual)
            dve.wait_ge(tile_free[0], freed(0, RING["out1"] + 16))
            dve.wait_ge(tile_free[1], freed(1, RING["out1"] + 16))
            dve.sem_inc(res_added, 16)
            norm_dve(dve, 1)
            dve.wait_ge(norm_rs, 2)
            dve.wait_ge(gb_in, 16)
            for i in range(NT):
                dve.scalar_tensor_tensor(out=xt[:, i, :], in0=hres[:, i, :], scalar=rstd(1, i), in1=gb[:, :],
                                         op0=ALU.mult, op1=ALU.mult).then_inc(xt_made, 1)
            for k in range(1, KD, 2):
                T = RING["xnffn"] + k
                dve.wait_ge(tile_full, T + 1)
                dve.tensor_copy(xtT[:, k, :], psg[:, T % 2, :]).then_inc(tile_free[T % 2], 1)
            dve.memset(hm[0:64, :], 0.0).then_inc(hm_cleared, 1)
            route(dve, link)

            def expert_dve(e, b, s_xgT_full, s_xgT, s_sg, s_hm):
                dve.wait_ge(s_xgT_full, e + 1)
                dve.tensor_copy(xgT[b][:, :, :].rearrange("p (h c) r -> p c h r", h=2),
                                psx[:, 2, :].rearrange("p (c h r) -> p c h r", h=2, r=BLK)).then_inc(s_xgT, 1)

            def expert_hidden(e, b, s_sg, s_hm):
                dve.wait_ge(s_sg, e + 1)
                dve.tensor_tensor(hm[64:128, :], psx[64:128, b, :], sg[64:128, :], ALU.mult).then_inc(s_hm, 1)

            expert_dve(0, 0, xgT_full, xgT_made, None, None)

            def expert_turn(e, b, last=False):
                if not last:
                    expert_dve(e + 1, 1 - b, xgT_full, xgT_made, None, None)
                expert_hidden(e, b, sg_made, hm_made)

            for e in range(2):
                expert_turn(e, e)
            with dve.Fori(1, NE // 2 - 1) as i:
                for b in range(2):
                    expert_turn(2 * i + b, b)
            expert_turn(NE - 2, 0)
            expert_turn(NE - 1, 1, last=True)
            more = dve.value_load(idx[0:1, 48:49], min_val=0, max_val=OVER)
            with dve.If(more > 0):
                with dve.Fori(0, OVER) as j:
                    expert_dve(NE + j, 0, xgT_full, xgT_made, None, None)
                    expert_hidden(NE + j, 0, sg_made, hm_made)
            for c in range(2 * NT):
                i = c // 2
                dve.wait_ge(rows_gathered[c], 16)
                if c % 2:
                    dve.wait_ge(combined, c)
                dve.scalar_tensor_tensor(out=hres[:, i, :], in0=yg[c][:, :], scalar=rt[:, 12, c:c + 1],
                                         in1=hres[:, i, :], op0=ALU.mult, op1=ALU.add).then_inc(combined, 1)
            block2_dve(dve, link)


def host_arrays(i):
    import numpy as np
    f = np.float32
    vec = np.zeros((P, NVEC), f)

    def put(name, a):
        vec[:, VEC[name][0]:VEC[name][1]] = a
    put("g_mix", i["g_mix"][0].reshape(8, P).T)
    put("b_dw", i["b_dw"][0].reshape(4, P).T)
    put("ln_g", i["ln_conv_g"][0].reshape(4, P).T)
    put("ln_b", i["ln_conv_b"][0].reshape(4, P).T)
    put("w_dw", i["w_dw"][0, :, 0, :].reshape(31, 4, P).transpose(2, 1, 0).reshape(P, 124))
    put("g_ffn", i["g_ffn"][0].reshape(8, P).T)
    put("mix_gain", i["mix_norm_gain_2"][0].reshape(8, P).T)
    put("ffn_gain", i["ffn_norm_gain_2"][0].reshape(8, P).T)
    put("conv2", i["gdn_conv_w_2"][0].reshape(4, 12, P).transpose(2, 1, 0).reshape(P, 48))
    put("gdn_gain", i["gdn_out_norm_gain_2"][0][:, None])
    vec[32:36, VEC["a_log"][0]] = i["gdn_a_log_2"][0]
    vec[32:36, VEC["dt_bias"][0]] = i["gdn_dt_bias_2"][0]
    small = np.zeros((D, P), f)
    small[:, 0:4] = i["w_in_2"][0][:, 2048:2052]
    small[:, 32:36] = i["w_in_2"][0][:, 2052:2056]
    small[:, 64:88] = i["w_in_2"][0][:, 3336:3360]
    a, b = np.arange(P)[:, None], np.arange(P)[None, :]
    same = a // CHUNK == b // CHUNK
    gmask = [same & (a < b), same & (a <= b)]
    for l in range(LEVELS):
        n = 2 ** l
        gmask.append((a // (2 * n) == b // (2 * n)) & (a // n % 2 == 0) & (b // n % 2 == 1))
    gmask = np.stack(gmask, 1).astype(f)
    sel = np.zeros((P, GH, P), f)
    for h in range(GH):
        sel[h::32, h, :] = 1.0
    half = 8
    inv = (np.float32(500000.0) ** (-np.arange(half, dtype=f) / half)).astype(f)
    ang = np.arange(SEQ, dtype=f)[None, :] * inv[:, None]
    cos, sin = np.ones((64, SEQ), f), np.zeros((64, SEQ), f)
    cos[0:16] = np.tile(np.cos(ang), (2, 1))
    sin[0:16] = np.tile(np.sin(ang), (2, 1))
    rot = np.zeros((P, P), f)
    for s in (0, 64):
        for m in range(half):
            rot[s + m + half, s + m] = -1.0
            rot[s + m, s + m + half] = 1.0
    tok = np.arange(SEQ).reshape(NT, P).T
    cmask = np.where(np.arange(31)[None, None, :] * 16 + 31 <= tok[:, :, None], 0.0, NEG).astype(f)
    q = np.arange(P)[:, None]
    rel = P + q - np.arange(256)[None, :]
    relneg = np.where((rel >= 0) & (rel < P), -rel, NEG).astype(f)
    return {
        "x": i["x"][0], "vec": vec, "ident": np.eye(P, dtype=f), "relneg": relneg, "sinks": i["sinks"],
        "gmask": gmask, "sel": sel, "chunk_go": (np.arange(SEQ) % CHUNK != 0).astype(f)[None],
        "cos": np.tile(cos, (2, 1)), "sin": np.tile(sin, (2, 1)), "rot": rot, "cmask": cmask,
        "dmask": np.where(b <= a, 0.0, NEG).astype(f), "rowvis": (np.arange(P) >= 31).astype(f)[:, None],
        "pos": np.stack([i[n][0].reshape(16, P).T for n in ("cmp_pos_k_2", "cmp_pos_v_2")], 1),
        "w2": np.concatenate([i["cmp_w2_k_2"][0], i["cmp_w2_k_2"][0], i["cmp_w2_v_2"][0]], axis=1),
        "cmp_w1_k_2": i["cmp_w1_k_2"][0].reshape(2048, P), "cmp_w1_v_2": i["cmp_w1_v_2"][0].reshape(2048, P),
        "w_small_2": small, "w_in_2": i["w_in_2"][0], "w_branch_gdn_2": i["w_branch_gdn_2"][0],
        "w_branch_nsa_2": i["w_branch_nsa_2"][0], "w_out_2": i["w_out_2"][0], "w_gate_up_2": i["w_gate_up_2"][0],
        "w_down_2": i["w_down_2"][0], "g_final_row": i["g_final"][None], "final_gain_row": i["final_norm_gain_2"][None],
        "tri": (np.arange(P)[:, None] < np.arange(P)[None, :]).astype(f),
        "desc": np.broadcast_to(32 - np.arange(32, dtype=f), (P, 32)),
        "w_router": np.concatenate([i["w_group"][0], i["w_expert"][0]], axis=1),
        "b_router": np.concatenate([i["b_group"][0], i["b_expert"][0]])[None],
        "g_ffn_row": i["g_ffn"], "w_gate": i["w_gate"][0], "w_up": i["w_up"][0], "w_down": i["w_down"][0],
        "w_in": i["w_in"][0], "w_conv_out": i["w_conv_out"][0], "w_attn_out": i["w_attn_out"][0], "w_out": i["w_out"][0],
    }


def kernel(**inputs):
    import numpy as np
    import concourse.bacc as bacc
    from concourse.bass_utils import run_bass_kernel_spmd

    laid = host_arrays({k: np.asarray(v) for k, v in inputs.items()})
    nc = bacc.Bacc("TRN2", target_bir_lowering=False, num_devices=1)
    arrays, t = {}, {}
    for name, a in laid.items():
        arrays[f"in_{name}"] = np.ascontiguousarray(a)
        t[name] = nc.dram_tensor(f"in_{name}", a.shape, mybir.dt.from_np(a.dtype), kind="ExternalInput").ap()
    t["out"] = nc.dram_tensor("out_0", (SEQ, D), F32, kind="ExternalOutput").ap()
    program(nc, t)
    r = run_bass_kernel_spmd(nc, [arrays], core_ids=[0])
    return r.results[0]["out_0"].reshape(1, SEQ, D)
```
